# Optimizing a Trainium2 kernel written in Bass

```python
import jax, jax.numpy as jnp
from jax import lax
import numpy as np

D_MODEL = 1024
BATCH = 1
SEQ = 512
DEPTH = 1

HEAD_DIM = 64
N_ATTN_HEADS = 8
ATTN_WIDTH = N_ATTN_HEADS * HEAD_DIM
N_CONV_GROUPS = 8
CONV_WIDTH = D_MODEL - ATTN_WIDTH
CONV_K = 3
IN_WIDTH = 3 * ATTN_WIDTH + 3 * CONV_WIDTH
DILATED_BRANCHES = ((128, 1), (512, 4), (2048, 16))
MAX_HALF = max(w // 2 for w, _ in DILATED_BRANCHES)
Q_BLOCK = 128
N_EXPERTS = 32
TOP_K = 4
D_FF = D_MODEL
SWIGLU_ALPHA = 1.702
SWIGLU_LIMIT = 7.0
EXPERT_BLOCK = 256
RMS_EPS = 1e-5
NEG_INF = -1e30

kernel_name = "hybrid_dilated_attn_shortconv_moe_encoder"

def rmsnorm(x, g):
    xf = x.astype(jnp.float32)
    y = xf * lax.rsqrt(jnp.mean(xf * xf, axis=-1, keepdims=True) + RMS_EPS)
    return (y * g.astype(jnp.float32)).astype(g.dtype)

def alibi_slopes(n_heads):
    return jnp.exp2(-8.0 * jnp.arange(1, n_heads + 1, dtype=jnp.float32) / n_heads)

def dilated_branch(qb, kp, vp, mp, q0, half, dil, slopes):
    B, H, QB, Dh = qb.shape
    n = half // dil
    L = QB + 2 * half
    A, C = QB // dil, L // dil
    start = q0 + (MAX_HALF - half)
    kb = lax.dynamic_slice_in_dim(kp, start, L, axis=2).reshape(B, H, C, dil, Dh)
    vb = lax.dynamic_slice_in_dim(vp, start, L, axis=2).reshape(B, H, C, dil, Dh)
    mb = lax.dynamic_slice_in_dim(mp, start, L, axis=0).reshape(C, dil).T
    qr = qb.reshape(B, H, A, dil, Dh)
    s = jnp.einsum('bhard,bhcrd->bhrac', qr, kb).astype(jnp.float32) * (HEAD_DIM ** -0.5)
    rel = jnp.arange(C)[None, :] - jnp.arange(A)[:, None] - n
    dist = (jnp.abs(rel) * dil).astype(jnp.float32)
    valid = (jnp.abs(rel) <= n)[None] & mb[:, None, :]
    s = jnp.where(valid, s - slopes[:, None, None, None] * dist, NEG_INF)
    m = jnp.max(s, axis=-1, keepdims=True)
    p = jnp.exp(s - m)
    den = jnp.sum(p, axis=-1)
    den_t = den.transpose(0, 1, 3, 2)
    o = jnp.einsum('bhrac,bhcrd->bhard', p, vb.astype(jnp.float32)) / den_t[..., None]
    lse = (m[..., 0].transpose(0, 1, 3, 2) + jnp.log(den_t)).reshape(B, H, QB)
    return o.reshape(B, H, QB, Dh), lse

def dilated_attention(q, k, v, slopes):
    B, H, S, Dh = q.shape
    pad = ((0, 0), (0, 0), (MAX_HALF, MAX_HALF), (0, 0))
    kp = jnp.pad(k, pad)
    vp = jnp.pad(v, pad)
    mp = jnp.pad(jnp.ones((S,), dtype=bool), MAX_HALF)

    def block(q0):
        qb = lax.dynamic_slice_in_dim(q, q0, Q_BLOCK, axis=2)
        outs, lses = [], []
        for window, dil in DILATED_BRANCHES:
            o, lse = dilated_branch(qb, kp, vp, mp, q0, window // 2, dil, slopes)
            outs.append(o)
            lses.append(lse)
        w = jax.nn.softmax(jnp.stack(lses), axis=0)
        return jnp.einsum('gbhq,gbhqd->bhqd', w, jnp.stack(outs))

    q0s = jnp.arange(S // Q_BLOCK, dtype=jnp.int32) * Q_BLOCK
    o = lax.map(block, q0s)
    return o.transpose(1, 0, 3, 2, 4).reshape(B, S, H * Dh)

def short_gated_conv(gb, gc, u, conv_w):
    z = gc * u
    zc = lax.conv_general_dilated(
        z, conv_w[:, None, :], window_strides=(1,),
        padding=((CONV_K // 2, CONV_K // 2),),
        dimension_numbers=('NWC', 'WIO', 'NWC'),
        feature_group_count=CONV_WIDTH)
    return gb * zc

def moe_ffn(h, w_router, b_router, w_gate_up, b_gate_up, w_down, b_down):
    B, S, D = h.shape
    T = B * S
    xf = h.reshape(T, D)
    logits = (xf @ w_router).astype(jnp.float32) + b_router.astype(jnp.float32)
    top_val, top_idx = lax.top_k(logits, TOP_K)
    gates = jax.nn.softmax(top_val, axis=-1)
    TK = T * TOP_K
    e_flat = top_idx.reshape(TK)
    tok_flat = jnp.arange(TK, dtype=jnp.int32) // TOP_K
    g_flat = gates.reshape(TK)
    order = jnp.argsort(e_flat)
    e_s, tok_s, g_s = e_flat[order], tok_flat[order], g_flat[order]
    counts = jnp.bincount(e_flat, length=N_EXPERTS)
    padded = (counts + EXPERT_BLOCK - 1) // EXPERT_BLOCK * EXPERT_BLOCK
    pad_end = jnp.cumsum(padded)
    pad_start = pad_end - padded
    grp_start = jnp.cumsum(counts) - counts
    dest = pad_start[e_s] + jnp.arange(TK, dtype=jnp.int32) - grp_start[e_s]
    n_blocks = -(-TK // EXPERT_BLOCK) + N_EXPERTS
    P = n_blocks * EXPERT_BLOCK
    buf_tok = jnp.zeros((P,), jnp.int32).at[dest].set(tok_s)
    buf_gate = jnp.zeros((P,), jnp.float32).at[dest].set(g_s)
    blk_exp = jnp.clip(jnp.searchsorted(pad_end, jnp.arange(n_blocks) * EXPERT_BLOCK,
                                        side='right'), 0, N_EXPERTS - 1)

    def expert_block(args):
        tok, g, e = args
        xb = xf[tok]
        hu = xb @ w_gate_up[e] + b_gate_up[e]
        a = jnp.minimum(hu[:, :D_FF], SWIGLU_LIMIT)
        lin = jnp.clip(hu[:, D_FF:], -SWIGLU_LIMIT, SWIGLU_LIMIT)
        act = a * jax.nn.sigmoid(SWIGLU_ALPHA * a) * (lin + 1)
        return (act @ w_down[e] + b_down[e]) * g[:, None].astype(xb.dtype)

    out = lax.map(expert_block, (buf_tok.reshape(n_blocks, EXPERT_BLOCK),
                                 buf_gate.reshape(n_blocks, EXPERT_BLOCK), blk_exp))
    y = jax.ops.segment_sum(out.reshape(P, D), buf_tok, num_segments=T)
    return y.reshape(B, S, D).astype(h.dtype)

def setup_inputs(seed: int = 0) -> dict:
    key = jax.random.key(seed)
    ks = jax.random.split(key, 16)
    f32 = jnp.float32

    def gain(k, n):
        return jnp.ones((DEPTH, n), f32) + 0.02 * jax.random.normal(k, (DEPTH, n), f32)

    return {
        "x": jax.random.normal(ks[0], (BATCH, SEQ, D_MODEL), f32),
        "mix_norm_g": gain(ks[1], D_MODEL),
        "w_in": jax.random.normal(ks[2], (DEPTH, D_MODEL, IN_WIDTH), f32) * D_MODEL ** -0.5,
        "conv_w": jax.random.normal(ks[3], (DEPTH, CONV_K, CONV_WIDTH), f32) * CONV_K ** -0.5,
        "attn_out_norm_g": gain(ks[4], ATTN_WIDTH),
        "conv_out_norm_g": gain(ks[5], CONV_WIDTH),
        "w_out": jax.random.normal(ks[6], (DEPTH, D_MODEL, D_MODEL), f32) * D_MODEL ** -0.5,
        "ffn_norm_g": gain(ks[7], D_MODEL),
        "w_router": jax.random.normal(ks[8], (DEPTH, D_MODEL, N_EXPERTS), f32) * D_MODEL ** -0.5,
        "b_router": 0.01 * jax.random.normal(ks[9], (DEPTH, N_EXPERTS), f32),
        "w_gate_up": jax.random.normal(ks[10], (DEPTH, N_EXPERTS, D_MODEL, 2 * D_FF), f32) * D_MODEL ** -0.5,
        "b_gate_up": 0.01 * jax.random.normal(ks[11], (DEPTH, N_EXPERTS, 2 * D_FF), f32),
        "w_down": jax.random.normal(ks[12], (DEPTH, N_EXPERTS, D_FF, D_MODEL), f32) * D_FF ** -0.5,
        "b_down": 0.01 * jax.random.normal(ks[13], (DEPTH, N_EXPERTS, D_MODEL), f32),
        "final_norm_g": jnp.ones((D_MODEL,), f32) + 0.02 * jax.random.normal(ks[14], (D_MODEL,), f32),
    }

def reference(x, mix_norm_g, w_in, conv_w, attn_out_norm_g, conv_out_norm_g, w_out,
              ffn_norm_g, w_router, b_router, w_gate_up, b_gate_up, w_down, b_down,
              final_norm_g):
    B, S, _ = x.shape
    slopes = alibi_slopes(N_ATTN_HEADS)
    splits = [int(s) for s in np.cumsum([ATTN_WIDTH] * 3 + [CONV_WIDTH] * 2)]
    for l in range(DEPTH):
        h = rmsnorm(x, mix_norm_g[l])
        proj = h @ w_in[l]
        q, k, v, gb, gc, u = jnp.split(proj, splits, axis=-1)

        def heads(t):
            return t.reshape(B, S, N_ATTN_HEADS, HEAD_DIM).transpose(0, 2, 1, 3)

        attn = dilated_attention(heads(q), heads(k), heads(v), slopes)
        conv = short_gated_conv(gb, gc, u, conv_w[l])
        merged = jnp.concatenate([rmsnorm(attn, attn_out_norm_g[l]),
                                  rmsnorm(conv, conv_out_norm_g[l])], axis=-1)
        x = x + merged @ w_out[l]
        x = x + moe_ffn(rmsnorm(x, ffn_norm_g[l]), w_router[l], b_router[l],
                        w_gate_up[l], b_gate_up[l], w_down[l], b_down[l])
    return rmsnorm(x, final_norm_g)


_drawn_inputs = setup_inputs


def setup_inputs(seed=0):
    import zlib

    import numpy as np

    out = dict(_drawn_inputs(seed))
    spreads = {}
    factors = {'b_gate_up': 8.0, 'b_down': 8.0, 'final_norm_g': 2.873}
    for name, (base, spread) in spreads.items():
        noise = np.random.default_rng([zlib.crc32(name.encode()), seed]).standard_normal(out[name].shape)
        drawn = base * np.exp(spread * noise) if base else spread * noise
        out[name] = __import__('jax').numpy.asarray(drawn.astype(out[name].dtype))
    for name, factor in factors.items():
        out[name] = (out[name] * factor).astype(out[name].dtype)
    return out
```

```python
from contextlib import ExitStack
import math

import concourse.bass as bass
from concourse import mybir

P = 128
F32 = mybir.dt.float32
F32R = mybir.dt.float32r
I32 = mybir.dt.int32
U32 = mybir.dt.uint32
ALU = mybir.AluOpType
ACT = mybir.ActivationFunctionType
AX = mybir.AxisListType

SEQ, D_MODEL = 512, 1024
TT = SEQ // P
KD = D_MODEL // P
HEADS, HEAD_DIM = 8, 64
AW = HEADS * HEAD_DIM
CW = D_MODEL - AW
NA, NC_ = AW // P, CW // P
BRANCHES = ((128, 1), (512, 4), (2048, 16))
E, TOPK = 32, 4
D_FF = D_MODEL
EPS = 1e-5
LIMIT, ALPHA = 7.0, 1.702
CHUNK = 2048
RAW_FRONT, SPLIT_FRONT = 4, 2
RAW, SPLIT = 6, 3
GU_CHUNKS = D_MODEL // P
DN_CHUNKS = D_FF // (2 * P)
JOB = GU_CHUNKS + DN_CHUNKS
ROWS = E * SEQ
NONE = 65535
MASKED = -1e30


def front_chunks():
    q, k, v, gb, gc, u = (AW // P * i for i in range(6))
    qk = [("qk", q + p, k + p) for p in range(NA)]
    conv = [("conv", gb, gc), ("conv", u, u + 1), ("conv", gb + 1, gc + 1),
            ("conv", gb + 2, gc + 2), ("conv", u + 2, u + 3), ("conv", gb + 3, gc + 3)]
    return [qk[0], ("v", v, v + 1), ("v", v + 2, v + 3), qk[1], conv[0], qk[2], conv[1], qk[3],
            conv[2], conv[3], conv[4], conv[5]]


CONV_TILES = [("gb", 0), ("gc", 0), ("u", 0), ("u", 1), ("gb", 1), ("gc", 1),
              ("gb", 2), ("gc", 2), ("u", 2), ("u", 3), ("gb", 3), ("gc", 3)]
CONV_DONE = {2: 0, 5: 1, 8: 2, 11: 3}


def build(nc, x, mix_norm_g, w_in, conv_w, attn_out_norm_g, conv_out_norm_g, w_out, ffn_norm_g,
          w_router, b_router, w_gate_up, b_gate_up, w_down, b_down, final_norm_g, out):
    chunks = front_chunks()
    N_IN = len(chunks)
    N_FRONT = N_IN + D_MODEL // (2 * P)
    tiles_of = [TT if c[0] == "v" else 2 for c in chunks]
    first_tile = [sum(tiles_of[:i]) for i in range(N_IN + 1)]

    xn_rows = nc.dram_tensor("xn_rows", (SEQ, D_MODEL), F32, kind="Internal").ap()
    lists = nc.dram_tensor("lists", (ROWS, 4), U32, kind="Internal").ap()
    y_rows = nc.dram_tensor("y_rows", (SEQ * TOPK, D_MODEL), F32, kind="Internal").ap()

    ctx = ExitStack()

    def sb(name, shape, dt=F32):
        return ctx.enter_context(nc.sbuf_tensor(name, shape, dt))

    def sem(name):
        return ctx.enter_context(nc.semaphore(name))

    def overlay(offset, *tensors):
        with ExitStack() as c:
            if offset:
                c.enter_context(nc.sbuf_tensor(f"before_{tensors[0][0]}", [P, offset // 4], F32))
            got = [c.enter_context(nc.sbuf_tensor(n, s, d)) for n, s, d in tensors]
        return got if len(got) > 1 else got[0]

    with ctx:
        raw01 = sb("raw01", [P, RAW_FRONT, CHUNK])
        hi01 = sb("hi01", [P, SPLIT_FRONT, CHUNK], F32R)
        lo01 = sb("lo01", [P, SPLIT_FRONT, CHUNK], F32R)
        ident = sb("ident", [P, P])
        g_mix = sb("g_mix", [P, KD])
        g_merge = sb("g_merge", [P, KD])
        g_ffn = sb("g_ffn", [P, KD])
        conv_c = sb("conv_c", [P, 3, NC_])
        stats = sb("stats", [P, 64])
        ss_x, std_x, rstd_x = (stats[:, TT * i:TT * i + TT] for i in range(3))
        ss_g, std_g, rstd_g = (stats[:, 16 + 8 * i:24 + 8 * i] for i in range(3))
        ss_1, std_1, rstd_1 = (stats[:, 40 + TT * i:44 + TT * i] for i in range(3))
        ss_f, std_f, rstd_f = (stats[:, 52 + TT * i:56 + TT * i] for i in range(3))
        ss_s = sb("ss_s", [P, TT, KD])
        max_s = sb("max_s", [P, HEADS * TT])
        neg_max = sb("neg_max", [P, HEADS * TT])
        den = sb("den", [P, HEADS * TT])
        rden = sb("rden", [P, HEADS * TT])
        ones = sb("ones", [P, P])
        sel_all = sb("sel_all", [2 * E, E])
        sel_gu = sb("sel_gu", [2 * E, P], F32R)
        sel_dn = sb("sel_dn", [2 * E, P], F32R)
        gather_list = sb("gather_list", [P, 4], U32)
        scatter_list = sb("scatter_list", [P, 4], U32)
        extra_sb = sb("extra_sb", [P, 1], I32)
        g_ffn_row = sb("g_ffn_row", [P, D_MODEL])
        w_r = sb("w_r", [P, KD, E])
        b_r = sb("b_r", [P, E])

        K, W = 1024, 896
        merged = overlay(0, ("merged", [P, KD, SEQ], F32))
        x_scaled = overlay(0, ("x_scaled", [P, TT, D_MODEL], F32))
        xnT_hi, xnT_lo = overlay(16 * K, ("xnT_hi", [P, KD, SEQ], F32R), ("xnT_lo", [P, KD, SEQ], F32R))
        qk_hi, qk_lo = overlay(48 * K, ("qk_hi", [P, 2, 2, SEQ], F32R), ("qk_lo", [P, 2, 2, SEQ], F32R))
        v_hi, v_lo = overlay(64 * K, ("v_hi", [P, TT, AW], F32R), ("v_lo", [P, TT, AW], F32R))
        x_sb = overlay(64 * K, ("x_sb", [P, TT, D_MODEL], F32))
        probs, pT_hi, pT_lo = overlay(80 * K, ("probs", [P, TT, SEQ], F32), ("pT_hi", [P, TT, SEQ], F32R),
                                      ("pT_lo", [P, TT, SEQ], F32R))
        diff, step4, step16, seen, seen_b = overlay(
            80 * K, ("diff", [P, W], I32), ("step4", [P, W], I32), ("step16", [P, W], I32),
            ("seen", [P, W], F32), ("seen_b", [P, W], F32))
        absd, log_m, bias_h, gb_sb, gc_sb, u_sb, z_sb, sq_sb = overlay(
            104 * K, ("absd", [P, W], F32), ("log_m", [P, W], F32), ("bias_h", [P, W], F32),
            ("gb_sb", [P, SEQ], F32), ("gc_sb", [P, SEQ], F32), ("u_sb", [P, 2, SEQ], F32),
            ("z_sb", [P, SEQ + 2], F32), ("sq_sb", [P, 2, SEQ], F32))
        mT_hi, mT_lo = overlay(16 * K, ("mT_hi", [P, KD, SEQ], F32R), ("mT_lo", [P, KD, SEQ], F32R))
        x1 = overlay(48 * K, ("x1", [P, TT, D_MODEL], F32))
        x1T = overlay(64 * K, ("x1T", [P, KD, SEQ], F32))
        xn = overlay(80 * K, ("xn", [P, 2, D_MODEL], F32))
        (logits, top_v, top_i, top_f, gexp, gsum, ex_e, chosen, chosen_p, mask, rank, dest_f, dest, entry,
         iota_e, base_e, tok_i, before, cnt_f, empty) = overlay(
            88 * K, ("logits", [P, TT, E], F32), ("top_v", [P, TT, 8], F32), ("top_i", [P, TT, 8], U32),
            ("top_f", [P, TT, TOPK], F32), ("gexp", [P, TT, TOPK], F32), ("gsum", [P, 2, TT], F32),
            ("ex_e", [P, TT, TOPK], F32), ("chosen", [P, TT, TOPK, E], F32),
            ("chosen_p", [P, TT, TOPK, E], F32), ("mask", [P, TT, E], F32), ("rank", [P, TT, E], F32),
            ("dest_f", [P, TT * TOPK], F32), ("dest", [P, TT * TOPK], U32),
            ("entry", [P, TT * TOPK, 4], U32), ("iota_e", [P, E], F32), ("base_e", [P, E], F32),
            ("tok_i", [P, 2, TT * TOPK], I32), ("before", [P, P], F32), ("cnt_f", [P, 4], F32),
            ("empty", [P, ROWS // P * 4], U32))
        hi2, lo2 = overlay(0, ("hi2", [P, CHUNK], F32R), ("lo2", [P, CHUNK], F32R))
        xT_hi, xT_lo, aT_hi, aT_lo = overlay(
            16 * K, ("xT_hi", [P, KD, P], F32R), ("xT_lo", [P, KD, P], F32R),
            ("aT_hi", [P, KD, P], F32R), ("aT_lo", [P, KD, P], F32R))
        x_got, gate_in, lin_in, sig_in = overlay(
            32 * K, ("x_got", [P, D_MODEL], F32), ("gate_in", [P, D_FF], F32),
            ("lin_in", [P, D_FF], F32), ("sig_in", [P, D_FF], F32))
        y_out, b_raw = overlay(64 * K, ("y_out", [P, D_MODEL], F32), ("b_raw", [2 * E, 3 * D_FF], F32))
        b_hl, raw2 = overlay(98 * K, ("b_hl", [2 * E, 3 * D_FF], F32R), ("raw2", [P, 2, CHUNK], F32))
        g_fin_row = overlay(80 * K, ("g_fin_row", [P, D_MODEL], F32))

        bank = [ctx.enter_context(nc.psum_tensor(f"bank{i}", [P, 512], F32)) for i in range(8)]

        x_loaded = [sem(f"x_loaded{t}") for t in range(TT)]
        x_again = sem("x_again")
        params_loaded = sem("params_loaded")
        g_mix_loaded = sem("g_mix_loaded")
        front_loaded = [sem(f"front_loaded{i}") for i in range(RAW_FRONT)]
        consts_made = sem("consts_made")
        tables_made = sem("tables_made")
        pool_step, dve_step, act_step = sem("pool_step"), sem("dve_step"), sem("act_step")
        ss_x_ready, var_x_ready, std_x_ready = sem("ss_x_ready"), sem("var_x_ready"), sem("std_x_ready")
        rstd_x_ready, x_scaled_ready = sem("rstd_x_ready"), sem("x_scaled_ready")
        xT_turned, xnT_hi_ready, xnT_lo_ready = sem("xT_turned"), sem("xnT_hi_ready"), sem("xnT_lo_ready")
        front_hi, front_lo, mix_half_used = sem("front_hi"), sem("front_lo"), sem("mix_half_used")
        sums_taken = sem("sums_taken")
        proj_ready, proj_hi_ready, proj_taken = sem("proj_ready"), sem("proj_hi_ready"), sem("proj_taken")
        scores_ready, scores_taken = sem("scores_ready"), sem("scores_taken")
        max_ready, exp_ready, probs_ready = sem("max_ready"), sem("exp_ready"), sem("probs_ready")
        probs_turned, pT_hi_ready, pT_lo_ready = sem("probs_turned"), sem("pT_hi_ready"), sem("pT_lo_ready")
        heads_ready, heads_taken = sem("heads_ready"), sem("heads_taken")
        sq_attn_ready, sq_attn_summed = sem("sq_attn_ready"), sem("sq_attn_summed")
        conv_ready = sem("conv_ready")
        sq_conv_ready, sq_conv_summed = sem("sq_conv_ready"), sem("sq_conv_summed")
        var_g_ready, std_g_ready = sem("var_g_ready"), sem("std_g_ready")
        mT_hi_ready, mT_lo_ready = sem("mT_hi_ready"), sem("mT_lo_ready")
        mix_ready, mix_taken = sem("mix_ready"), sem("mix_taken")
        x1_turned, x1T_act_ready, x1T_dve_ready = sem("x1_turned"), sem("x1T_act_ready"), sem("x1T_dve_ready")
        router_ready = sem("router_ready")
        ss_1_ready, var_1_ready, std_1_ready, rstd_1_ready = (
            sem("ss_1_ready"), sem("var_1_ready"), sem("std_1_ready"), sem("rstd_1_ready"))
        xn_scaled, xn_ready, xn_stored = sem("xn_scaled"), sem("xn_ready"), sem("xn_stored")
        w_r_ready = sem("w_r_ready")
        gate_shift_ready, gate_exp_ready = sem("gate_shift_ready"), sem("gate_exp_ready")
        mask_ready, rank_ready = sem("mask_ready"), sem("rank_ready")
        entry_made, entry_ready = sem("entry_made"), sem("entry_ready")
        extra_ready = sem("extra_ready")
        lists_emptied, lists_ready = sem("lists_emptied"), sem("lists_ready")
        b_loaded, b_hi_ready, b_ready = sem("b_loaded"), sem("b_hi_ready"), sem("b_ready")
        w_loaded = [sem(f"w_loaded{i}") for i in range(RAW)]
        w_hi_ready, w_lo_ready, w_used = sem("w_hi_ready"), sem("w_lo_ready"), sem("w_used")
        gather_list_loaded, x_gathered = sem("gather_list_loaded"), sem("x_gathered")
        x_got_cleared = sem("x_got_cleared")
        got_turned, xT_hi_ready, xT_lo_ready = sem("got_turned"), sem("xT_hi_ready"), sem("xT_lo_ready")
        sel_gu_ready, sel_gu_used = sem("sel_gu_ready"), sem("sel_gu_used")
        sel_dn_ready, sel_dn_used = sem("sel_dn_ready"), sem("sel_dn_used")
        gu_clamped, sig_ready = sem("gu_clamped"), sem("sig_ready")
        lin_gated, act_ready = sem("lin_gated"), sem("act_ready")
        act_turned, aT_hi_ready, aT_lo_ready = sem("act_turned"), sem("aT_hi_ready"), sem("aT_lo_ready")
        y_half_ready, y_ready = sem("y_half_ready"), sem("y_ready")
        scatter_list_loaded, y_stored = sem("scatter_list_loaded"), sem("y_stored")
        g_fin_loaded = sem("g_fin_loaded")
        y_loaded = [sem(f"y_loaded{i}") for i in range(2)]
        y_added, ss_f_ready, var_f_ready, std_f_ready = (
            sem("y_added"), sem("ss_f_ready"), sem("var_f_ready"), sem("std_f_ready"))
        rstd_f_ready, out_scaled, out_ready, out_stored = (
            sem("rstd_f_ready"), sem("out_scaled"), sem("out_ready"), sem("out_stored"))

        def raw_slot(m):
            return raw01[:, m, :] if m < RAW_FRONT else raw2[:, m - RAW_FRONT, :]

        def hi_slot(m):
            return hi01[:, m, :] if m < SPLIT_FRONT else hi2[:, :]

        def lo_slot(m):
            return lo01[:, m, :] if m < SPLIT_FRONT else lo2[:, :]

        def gu_chunk(j, i):
            return i if isinstance(j, int) and j == 0 else (j - 1) * JOB + (GU_CHUNKS + i)

        def dn_chunk(j, i):
            return j * JOB + (2 * GU_CHUNKS + i)

        def last_dn_chunk(j, i):
            return (j * JOB) + (GU_CHUNKS + i)

        GU0 = [i for i in range(GU_CHUNKS)]
        GU = [GU_CHUNKS + i for i in range(GU_CHUNKS)]
        DN = [2 * GU_CHUNKS + i for i in range(DN_CHUNKS)]
        DN_LAST = [GU_CHUNKS + i for i in range(DN_CHUNKS)]
        assert JOB % RAW == 0 and JOB % SPLIT == 0

        def expert(j):
            return j % E if isinstance(j, int) else j & (E - 1)

        def round_(j):
            return j // E % TT if isinstance(j, int) else (j >> (E.bit_length() - 1)) & (TT - 1)

        def fixed(eng, value):
            return value if isinstance(value, int) else eng.snap(eng.to_reg(value))

        def is_split(i):
            return next(c[0] for n, c in enumerate(chunks) if i < first_tile[n + 1]) != "conv"

        def splits_to(i):
            return sum(is_split(n) for n in range(i + 1))

        def jobs_end(eng):
            eng.wait_ge(extra_ready, 1)
            extra = eng.value_load(extra_sb[0:1, 0:1], min_val=0, max_val=TT - 1)
            return eng.snap(extra * E + E)

        def wait_used(eng, s):
            if s < N_IN:
                eng.wait_ge(proj_ready, first_tile[s + 1])
            elif (s - N_IN) % 2 == 0:
                eng.wait_ge(mix_half_used, (s - N_IN) // 2 + 1)
            else:
                eng.wait_ge(mix_ready, 2 * TT * ((s - N_IN) // 2 + 1))

        block = ctx.enter_context(nc.Block())

        @block.sync
        def _(sp):
            for t in range(TT):
                sp.dma_start(x_sb[:, t, :], x[0, t * P:(t + 1) * P, :]).then_inc(x_loaded[t], 16)
            w_in_v = w_in[0].rearrange("(k p) n -> p k n", p=P)
            for s in range(N_FRONT):
                if s >= RAW_FRONT:
                    sp.wait_ge(front_hi, s - RAW_FRONT + 1)
                    sp.wait_ge(front_lo, s - RAW_FRONT + 1)
                slot = raw01[:, s % RAW_FRONT, :]
                for n in range(2):
                    if s < N_IN:
                        c = chunks[s][1 + n]
                        src = w_in_v[:, :, c * P:(c + 1) * P]
                        dst = slot.rearrange("p (k two n) -> p k two n", k=KD, two=2)[:, :, n, :]
                    else:
                        c = 2 * (s - N_IN) + n
                        src, dst = w_out[0, c * P:(c + 1) * P, :], slot[:, n * D_MODEL:(n + 1) * D_MODEL]
                    sp.dma_start(dst, src).then_inc(front_loaded[s % RAW_FRONT], 16)

            def load_gu(e, i, m, slot_no):
                wait_slot(m, slot_no)
                sp.dma_start(raw_slot(slot_no % RAW), w_gate_up[0, e, i * P:(i + 1) * P, :])\
                  .then_inc(w_loaded[slot_no % RAW], 16)

            def load_dn(e, i, m, slot_no):
                wait_slot(m, slot_no)
                sp.dma_start(raw_slot(slot_no % RAW).rearrange("p (i n) -> p i n", i=2),
                             w_down[0, e, 2 * i * P:2 * (i + 1) * P, :].rearrange("(i p) n -> p i n", p=P))\
                  .then_inc(w_loaded[slot_no % RAW], 16)

            def wait_slot(m, slot_no):
                if not isinstance(m, int) or m >= RAW:
                    sp.wait_ge(w_hi_ready, m - (RAW - 1))
                    sp.wait_ge(w_lo_ready, m - (RAW - 1))
                elif m < RAW_FRONT:
                    s = N_IN + m
                    sp.wait_ge(front_hi, s + 1)
                    sp.wait_ge(front_lo, s + 1)
                elif m == RAW_FRONT:
                    sp.wait_ge(conv_ready, NC_)
                    sp.wait_ge(sq_attn_summed, NA)
                    sp.wait_ge(sq_conv_summed, NC_)
                    sp.wait_ge(scores_taken, HEADS * TT)

            def job(j):
                e, before_e = fixed(sp, expert(j)), fixed(sp, expert(j - 1))
                for i in range(GU_CHUNKS):
                    load_gu(e, i, gu_chunk(j, i), GU[i])
                for i in range(DN_CHUNKS):
                    load_dn(before_e, i, dn_chunk(j - 1, i), DN[i])

            for i in range(GU_CHUNKS):
                load_gu(0, i, i, GU0[i])
            job(1)
            end = jobs_end(sp)
            with sp.Fori(2, end) as j:
                job(j)
            for i in range(DN_CHUNKS):
                load_dn(E - 1, i, last_dn_chunk(end - 1, i), DN_LAST[i])

            sp.wait_ge(xn_stored, 16 * TT)
            sp.dma_start(g_fin_row[:, :], final_norm_g.partition_broadcast(P)).then_inc(g_fin_loaded, 16)
            stored, used = fixed(sp, end * 16), fixed(sp, end * JOB)
            sp.wait_ge(y_stored, stored)
            sp.wait_ge(w_hi_ready, used)
            sp.wait_ge(w_lo_ready, used)
            for t in range(TT):
                if t >= 2:
                    sp.wait_ge(y_added, t - 1)
                b = t % 2
                sp.dma_start(raw01[:, 2 * b:2 * b + 2, :].rearrange("p a n -> p (a n)"),
                             y_rows[t * P * TOPK:(t + 1) * P * TOPK, :].rearrange("(p k) n -> p (k n)", k=TOPK))\
                  .then_inc(y_loaded[b], 16)
            for t in range(TT):
                sp.wait_ge(out_ready, t + 1)
                sp.dma_start(out[0, t * P:(t + 1) * P, :], x1[:, t, :]).then_inc(out_stored, 16)
            sp.wait_ge(out_stored, 16 * TT)

        @block.gpsimd
        def _(pool):
            steps = 0

            def made(ins):
                nonlocal steps
                steps += 1
                ins.then_inc(pool_step, 1)
                pool.wait_ge(pool_step, steps)

            pool.iota(diff[:, :], pattern=[[-1, W]], base=(TT - 1) * P, channel_multiplier=1).then_inc(consts_made, 1)
            pool.memset(ident[:, :], 0.0).then_inc(pool_step, 1)
            steps += 1
            pool.wait_ge(pool_step, steps)
            pool.affine_select(out=ident[:, :], in_=ident[:, :], compare_op=ALU.not_equal, fill=1.0, base=0,
                               pattern=[[-1, P]], channel_multiplier=1).then_inc(consts_made, 1)
            pool.memset(ones[:, :], 1.0).then_inc(consts_made, 1)
            pool.memset(z_sb[:, :], 0.0).then_inc(consts_made, 1)
            made(pool.memset(sel_all[:, :], 0.0))
            for half in range(2):
                made(pool.affine_select(out=sel_all[:, :], in_=sel_all[:, :], compare_op=ALU.not_equal, fill=1.0,
                                        base=-half * E, pattern=[[-1, E]], channel_multiplier=1))
            per_p = [(g_merge[:, 0:NA], attn_out_norm_g[0].rearrange("(k p) -> p k", p=P)),
                     (g_merge[:, NA:KD], conv_out_norm_g[0].rearrange("(k p) -> p k", p=P)),
                     (g_ffn[:, :], ffn_norm_g[0].rearrange("(k p) -> p k", p=P)),
                     (conv_c[:, 0, :], conv_w[0, 0].rearrange("(k p) -> p k", p=P)),
                     (conv_c[:, 1, :], conv_w[0, 1].rearrange("(k p) -> p k", p=P)),
                     (conv_c[:, 2, :], conv_w[0, 2].rearrange("(k p) -> p k", p=P)),
                     (g_ffn_row[:, :], ffn_norm_g[0].partition_broadcast(P)),
                     (b_r[:, :], b_router[0].partition_broadcast(P)),
                     (w_r[:, :, :], w_router[0].rearrange("(k p) e -> p k e", p=P))]
            for dst, src in per_p:
                pool.dma_start(dst, src, allow_slow_non_contiguous=True).then_inc(params_loaded, 16)

            pool.wait_ge(scores_ready, HEADS * TT)
            for t in range(TT):
                pool.dma_start(x1[:, t, :], x[0, t * P:(t + 1) * P, :]).then_inc(x_again, 16)

            pool.wait_ge(heads_ready, HEADS)
            made(pool.memset(empty[:, :], NONE))
            pool.dma_start(lists.rearrange("(p r) c -> p (r c)", p=P), empty[:, :]).then_inc(lists_emptied, 16)
            pool.iota(iota_e[:, :], pattern=[[1, E]], base=0, channel_multiplier=0,
                      allow_small_or_imprecise_dtypes=True).then_inc(consts_made, 1)
            pool.iota(base_e[:, :], pattern=[[SEQ, E]], base=0, channel_multiplier=0,
                      allow_small_or_imprecise_dtypes=True).then_inc(consts_made, 1)
            made(pool.memset(before[:, :], 1.0))
            pool.affine_select(out=before[:, :], in_=before[:, :], compare_op=ALU.is_gt, fill=0.0, base=0,
                               pattern=[[1, P]], channel_multiplier=-1).then_inc(consts_made, 1)
            made(pool.memset(entry[:, :, :], 0))
            made(pool.iota(entry[:, :, 0].bitcast(I32), pattern=[[P, TT], [0, TOPK]], base=0, channel_multiplier=1))
            pool.iota(entry[:, :, 1].bitcast(I32), pattern=[[P * TOPK, TT], [1, TOPK]], base=0,
                      channel_multiplier=TOPK).then_inc(entry_made, 1)
            wait_used(pool, N_FRONT - 1)
            pool.memset(x_got[:, :], 0.0).then_inc(x_got_cleared, 1)

            last_place, last_row, last_token = pool.to_reg(ROWS - 1), pool.to_reg(SEQ * TOPK - 1), pool.to_reg(SEQ - 1)
            pool.wait_ge(lists_emptied, 16)
            pool.wait_ge(entry_made, 1)
            pool.wait_ge(entry_ready, 1)
            for n in range(TT * TOPK):
                pool.indirect_dma_start(out=lists, out_offset=bass.IndirectOffsetOnAxis(ap=dest[:, n:n + 1], axis=0),
                                        in_=entry[:, n, :], in_offset=None, bounds_check=last_place,
                                        oob_is_err=False).then_inc(lists_ready, 16)
            pool.wait_ge(lists_ready, 16 * TT * TOPK)

            def list_row(j):
                return fixed(pool, expert(j) * SEQ + round_(j) * P)

            def load_list(dst, row, done):
                pool.dma_start(dst[:, :], lists[bass.ds(row, P), :]).then_inc(done, 16)

            def gather(j):
                row, lists_, turns = list_row(j), fixed(pool, j * 16 + 16), fixed(pool, j * 2)
                if not (isinstance(j, int) and j == 0):
                    pool.wait_ge(x_gathered, j * 16)
                load_list(gather_list, row, gather_list_loaded)
                pool.wait_ge(x_got_cleared, 1)
                pool.wait_ge(xn_stored, 16 * TT)
                pool.wait_ge(gather_list_loaded, lists_)
                if not (isinstance(j, int) and j == 0):
                    pool.wait_ge(got_turned, turns)
                pool.indirect_dma_start(out=x_got[:, :], out_offset=None, in_=xn_rows,
                                        in_offset=bass.IndirectOffsetOnAxis(ap=gather_list[:, 0:1], axis=0),
                                        bounds_check=last_token, oob_is_err=False).then_inc(x_gathered, 16)

            def scatter(j):
                done = fixed(pool, j + 1)
                pool.wait_ge(lists_ready, 16 * TT * TOPK)
                pool.wait_ge(y_half_ready, done)
                pool.wait_ge(y_ready, done)
                pool.indirect_dma_start(out=y_rows, in_=y_out[:, :], in_offset=None,
                                        out_offset=bass.IndirectOffsetOnAxis(ap=scatter_list[:, 1:2], axis=0),
                                        bounds_check=last_row, oob_is_err=False).then_inc(y_stored, 16)

            def load_scatter_list(j):
                row = list_row(j)
                if not (isinstance(j, int) and j == 0):
                    pool.wait_ge(y_stored, j * 16)
                load_list(scatter_list, row, scatter_list_loaded)

            gather(0)
            gather(1)

            def job(j, first=False):
                gather(j + 1)
                if not first:
                    scatter(j - 2)
                load_scatter_list(j - 1)

            job(1, first=True)
            end = jobs_end(pool)
            with pool.Fori(2, end) as j:
                job(j)
            scatter(end - 2)
            load_scatter_list(end - 1)
            scatter(end - 1)
            pool.wait_ge(y_stored, end * 16)
            pool.wait_ge(x_gathered, end * 16 + 16)

        @block.scalar
        def _(act):
            act.dma_start(g_mix[:, :], mix_norm_g[0].rearrange("(k p) -> p k", p=P),
                          allow_slow_non_contiguous=True).then_inc(g_mix_loaded, 16)

            for t in range(TT):
                act.wait_ge(x_loaded[t], 16)
                act.activation(x_scaled[:, t, :], x_sb[:, t, :], ACT.Square, accum_out=ss_x[:, t:t + 1])\
                   .then_inc(ss_x_ready, 1)
            act.wait_ge(var_x_ready, 1)
            act.activation(std_x, std_x, ACT.Sqrt).then_inc(std_x_ready, 1)
            act.wait_ge(rstd_x_ready, 1)
            for t in range(TT):
                act.activation(x_scaled[:, t, :], x_sb[:, t, :], ACT.Copy, scale=rstd_x[:, t:t + 1])\
                   .then_inc(x_scaled_ready, 1)

            def split_front(s):
                act.wait_ge(front_loaded[s % RAW_FRONT], 32 * (s // RAW_FRONT + 1))
                if s >= SPLIT_FRONT:
                    wait_used(act, s - SPLIT_FRONT)
                act.activation(hi01[:, s % SPLIT_FRONT, :], raw01[:, s % RAW_FRONT, :], ACT.Copy)\
                   .then_inc(front_hi, 1)

            split_front(0)
            act.wait_ge(g_mix_loaded, 16)
            for k in range(KD):
                act.wait_ge(xT_turned, k + 1)
                act.activation(xnT_hi[:, k, :], bank[k][:, :], ACT.Copy, scale=g_mix[:, k:k + 1])\
                   .then_inc(xnT_hi_ready, 1)
            split_front(1)

            def take(s, n):
                i, kind = first_tile[s] + n, chunks[s][0]
                if kind == "conv":
                    return
                act.wait_ge(proj_ready, i + 1)
                if kind == "v":
                    dst, src = v_hi[:, n, (s - 1) * 2 * P:s * 2 * P], bank[i % 2][:, 0:2 * P]
                else:
                    dst, src = qk_hi[:, chunks[s][1] % 2, n, :], bank[i % 2][:, :]
                act.activation(dst, src, ACT.Copy).then_inc(proj_hi_ready, 1)

            for s in range(3):
                for n in range(tiles_of[s]):
                    take(s, n)
                split_front(s + 2)

            def take_head(h):
                half = slice(HEAD_DIM * (h % 2), HEAD_DIM * (h % 2) + HEAD_DIM)
                act.wait_ge(heads_ready, h + 1)
                act.activation(merged[half, h // 2, :], bank[6][half, :], ACT.Copy).then_inc(heads_taken, 1)
                if h % 2:
                    act.wait_ge(heads_taken, h + 1)
                    if h > 1:
                        act.wait_ge(sq_attn_summed, h // 2)
                    act.activation(sq_sb[:, 0, :], merged[:, h // 2, :], ACT.Square).then_inc(sq_attn_ready, 1)

            def square_conv(c):
                act.wait_ge(conv_ready, c + 1)
                if c:
                    act.wait_ge(sq_conv_summed, c)
                act.activation(sq_sb[:, 1, :], merged[:, NA + c, :], ACT.Square).then_inc(sq_conv_ready, 1)

            for h in range(HEADS):
                s = 3 + h
                if h:
                    split_front(s + 1)
                act.wait_ge(max_ready, h + 1)
                for t in range(TT):
                    act.activation(probs[:, t, :], probs[:, t, :], ACT.Exp, bias=neg_max[:, h * TT + t:h * TT + t + 1],
                                   scale=HEAD_DIM ** -0.5, accum_out=den[:, h * TT + t:h * TT + t + 1])\
                       .then_inc(exp_ready, 1)
                take(s, 0)
                if h:
                    take_head(h - 1)
                take(s, 1)
                for c in range(TT):
                    act.wait_ge(probs_turned, h * TT + c + 1)
                    act.activation(pT_hi[:, c, :], bank[4 + c % 2][:, :], ACT.Copy).then_inc(pT_hi_ready, 1)
                if h in (4, 6):
                    square_conv(h // 2 - 2)
            take_head(HEADS - 1)
            split_front(N_IN)
            square_conv(2)

            wait_used(act, N_IN - 1)
            act.wait_ge(params_loaded, 16 * 9)

            def split_merged(k):
                if k >= NA:
                    act.wait_ge(conv_ready, k - NA + 1)
                act.activation(mT_hi[:, k, :], merged[:, k, :], ACT.Copy, scale=g_merge[:, k:k + 1])\
                   .then_inc(mT_hi_ready, 1)

            act.wait_ge(heads_taken, HEADS)
            for k in range(NA):
                split_merged(k)
            split_front(N_IN + 1)
            square_conv(3)
            for k in range(NA, KD):
                split_merged(k)
            act.wait_ge(var_g_ready, 1)
            act.activation(std_g, std_g, ACT.Sqrt).then_inc(std_g_ready, 1)
            split_front(N_IN + 2)
            split_front(N_IN + 3)

            for t in range(TT):
                act.wait_ge(mix_taken, TT * 2 + 2 * t + 2)
                if t >= 2:
                    act.wait_ge(ss_1_ready, t - 1)
                act.activation(xn[:, t % 2, :], x1[:, t, :], ACT.Square, accum_out=ss_1[:, t:t + 1])\
                   .then_inc(ss_1_ready, 1)
                act.wait_ge(x1_turned, 2 * t + 1)
                act.activation(x1T[:, 0:TT, t * P:(t + 1) * P],
                               bank[2 * t][:, :].rearrange("p (k n) -> p k n", k=TT), ACT.Copy)\
                   .then_inc(x1T_act_ready, 1)
            act.wait_ge(var_1_ready, 1)
            act.activation(std_1, std_1, ACT.Sqrt).then_inc(std_1_ready, 1)
            act.wait_ge(rstd_1_ready, 1)
            for t in range(TT):
                if t >= 2:
                    act.wait_ge(xn_stored, 16 * t)
                else:
                    act.wait_ge(ss_1_ready, TT)
                if t == 2:
                    act.wait_ge(gate_shift_ready, 1)
                    act.activation(gexp[:, :, :], gexp[:, :, :], ACT.Exp).then_inc(gate_exp_ready, 1)
                act.activation(xn[:, t % 2, :], x1[:, t, :], ACT.Copy, scale=rstd_1[:, t:t + 1])\
                   .then_inc(xn_scaled, 1)
                act.wait_ge(xn_ready, t + 1)
                act.dma_start(xn_rows[t * P:(t + 1) * P, :], xn[:, t % 2, :]).then_inc(xn_stored, 16)
            act.wait_ge(router_ready, TT)
            for half in range(2):
                rows = slice(half * E, half * E + E)
                act.dma_start(b_raw[rows, 0:2 * D_FF], b_gate_up[0]).then_inc(b_loaded, 16)
                act.dma_start(b_raw[rows, 2 * D_FF:3 * D_FF], b_down[0]).then_inc(b_loaded, 16)
            act.wait_ge(b_loaded, 64)
            act.activation(b_hl[:, :], b_raw[:, :], ACT.Copy).then_inc(b_hi_ready, 1)

            def split(m, slot_no, loads):
                act.wait_ge(w_loaded[slot_no % RAW], loads * 16)
                if isinstance(m, int) and m < SPLIT:
                    wait_used(act, N_FRONT - 1)
                else:
                    act.wait_ge(w_used, m - (SPLIT - 1))
                act.activation(hi_slot(slot_no % SPLIT), raw_slot(slot_no % RAW), ACT.Copy).then_inc(w_hi_ready, 1)

            def gu(j, i):
                split(gu_chunk(j, i), GU[i], loads_of(j - 1, GU[i]))

            def dn(j, i):
                split(dn_chunk(j, i), DN[i], loads_of(j, DN[i]))

            def loads_of(jobs, slot_no):
                return jobs * (JOB // RAW) + (slot_no // RAW + 1)

            def turned(j, hi, bank_ready, hi_ready):
                for g in range(2):
                    act.wait_ge(bank_ready, j * 2 + (g + 1))
                    act.activation(hi[:, g * TT:(g + 1) * TT, :].rearrange("p k n -> p (k n)"), bank[6 + g][:, :],
                                   ACT.Copy).then_inc(hi_ready, 1)

            def sigmoid(j):
                act.wait_ge(gu_clamped, j * 2 + 1)
                if not (isinstance(j, int) and j == 0):
                    act.wait_ge(act_ready, j)
                act.activation(sig_in[:, :], gate_in[:, :], ACT.Sigmoid, scale=ALPHA).then_inc(sig_ready, 1)

            def take_y(j):
                act.wait_ge(scatter_list_loaded, j * 16 + 16)
                for g in range(2):
                    if g == 0:
                        act.wait_ge(w_used, y_chunks(j))
                    act.activation(y_out[:, g * 512:(g + 1) * 512], bank[4 + g][:, :], ACT.Copy,
                                   scale=scatter_list[:, 2:3].bitcast(F32)).then_inc(y_half_ready if g == 0 else y_ready, 1)

            def y_chunks(j):
                return j * JOB + (2 * GU_CHUNKS + DN_CHUNKS)

            for i in range(GU_CHUNKS):
                split(i, i, i // RAW + 1)
                if i == 1:
                    turned(0, xT_hi, got_turned, xT_hi_ready)

            def job(j, first=False):
                gu(j, 0)
                if first:
                    turned(1, xT_hi, got_turned, xT_hi_ready)
                sigmoid(j - 1)
                gu(j, 1)
                gu(j, 2)
                if not first:
                    take_y(j - 2)
                for i in range(3, 7):
                    gu(j, i)
                turned(j - 1, aT_hi, act_turned, aT_hi_ready)
                gu(j, 7)
                for i in range(3):
                    dn(j - 1, i)
                turned(j + 1, xT_hi, got_turned, xT_hi_ready)
                dn(j - 1, 3)

            job(1, first=True)
            end = jobs_end(act)
            with act.Fori(2, end) as j:
                job(j)
            last = end - 1
            sigmoid(last)
            take_y(end - 2)
            split(last_dn_chunk(last, 0), DN_LAST[0], loads_of(last, DN_LAST[0]))
            turned(last, aT_hi, act_turned, aT_hi_ready)
            for i in range(1, DN_CHUNKS):
                split(last_dn_chunk(last, i), DN_LAST[i], loads_of(last, DN_LAST[i]))
            act.wait_ge(scatter_list_loaded, end * 16)
            act.wait_ge(y_stored, end * 16 - 16)
            act.wait_ge(w_used, end * JOB)
            act.activation(y_out[:, 0:512], bank[4][:, :], ACT.Copy,
                           scale=scatter_list[:, 2:3].bitcast(F32)).then_inc(y_half_ready, 1)
            act.activation(y_out[:, 512:1024], bank[5][:, :], ACT.Copy,
                           scale=scatter_list[:, 2:3].bitcast(F32)).then_inc(y_ready, 1)

            for t in range(TT):
                act.wait_ge(y_added, t + 1)
                if t == 0:
                    act.wait_ge(y_stored, end * 16)
                else:
                    act.wait_ge(ss_f_ready, t)
                act.activation(y_out[:, :], x1[:, t, :], ACT.Square, accum_out=ss_f[:, t:t + 1]).then_inc(ss_f_ready, 1)
                act.wait_ge(var_f_ready, t + 1)
                act.activation(std_f[:, t:t + 1], std_f[:, t:t + 1], ACT.Sqrt).then_inc(std_f_ready, 1)
                act.wait_ge(rstd_f_ready, t + 1)
                act.activation(x1[:, t, :], x1[:, t, :], ACT.Copy, scale=rstd_f[:, t:t + 1]).then_inc(out_scaled, 1)

        @block.vector
        def _(dve):
            steps = 0

            def did(ins):
                nonlocal steps
                steps += 1
                ins.then_inc(dve_step, 1)
                dve.wait_ge(dve_step, steps)

            dve.wait_ge(consts_made, 1)
            did(dve.tensor_scalar(step4[:, :], diff[:, :], BRANCHES[1][1] - 1, None, ALU.bitwise_and))
            did(dve.tensor_scalar(step16[:, :], diff[:, :], BRANCHES[2][1] - 1, None, ALU.bitwise_and))
            did(dve.tensor_copy(absd[:, :], diff[:, :]))
            did(dve.scalar_tensor_tensor(absd[:, :], absd[:, :], -1.0, absd[:, :], ALU.mult, ALU.max))

            dve.wait_ge(ss_x_ready, TT)
            dve.tensor_scalar(std_x, ss_x, 1.0 / D_MODEL, EPS, ALU.mult, ALU.add).then_inc(var_x_ready, 1)
            dve.wait_ge(std_x_ready, 1)
            dve.reciprocal(rstd_x, std_x).then_inc(rstd_x_ready, 1)

            def split_front(s):
                dve.wait_ge(front_hi, s + 1)
                dve.wait_ge(front_loaded[s % RAW_FRONT], 32 * (s // RAW_FRONT + 1))
                if s >= SPLIT_FRONT:
                    wait_used(dve, s - SPLIT_FRONT)
                dve.tensor_tensor(lo01[:, s % SPLIT_FRONT, :], raw01[:, s % RAW_FRONT, :],
                                  hi01[:, s % SPLIT_FRONT, :], ALU.subtract).then_inc(front_lo, 1)

            split_front(0)
            dve.wait_ge(g_mix_loaded, 16)
            for k in range(KD):
                dve.wait_ge(xnT_hi_ready, k + 1)
                dve.scalar_tensor_tensor(xnT_lo[:, k, :], bank[k][:, :], g_mix[:, k:k + 1], xnT_hi[:, k, :],
                                         ALU.mult, ALU.subtract).then_inc(xnT_lo_ready, 1)
            split_front(1)

            def take(s, n):
                i, kind = first_tile[s] + n, chunks[s][0]
                if kind == "conv":
                    c = sum(x[0] == "conv" for x in chunks[:s]) * 2 + n
                    name, ch = CONV_TILES[c]
                    dst = {"gb": gb_sb[:, :], "gc": gc_sb[:, :], "u": u_sb[:, ch % 2, :]}[name]
                    dve.wait_ge(proj_ready, i + 1)
                    dve.tensor_copy(dst, bank[i % 2][:, :]).then_inc(proj_taken, 1)
                    if c in CONV_DONE:
                        dve.wait_ge(proj_taken, i + 1)
                        convolve(CONV_DONE[c])
                    return
                dve.wait_ge(proj_hi_ready, splits_to(i))
                if kind == "v":
                    cols = slice((s - 1) * 2 * P, s * 2 * P)
                    out_, src, hi = v_lo[:, n, cols], bank[i % 2][:, 0:2 * P], v_hi[:, n, cols]
                else:
                    b = chunks[s][1] % 2
                    out_, src, hi = qk_lo[:, b, n, :], bank[i % 2][:, :], qk_hi[:, b, n, :]
                dve.tensor_tensor(out_, src, hi, ALU.subtract).then_inc(proj_taken, 1)

            def convolve(c):
                dst = merged[:, NA + c, :]
                dve.wait_ge(consts_made, 4)
                did(dve.tensor_tensor(z_sb[:, 1:SEQ + 1], gc_sb[:, :], u_sb[:, c % 2, :], ALU.mult))
                did(dve.tensor_scalar(dst, z_sb[:, 0:SEQ], conv_c[:, 0, c:c + 1], None, ALU.mult))
                did(dve.scalar_tensor_tensor(dst, z_sb[:, 1:SEQ + 1], conv_c[:, 1, c:c + 1], dst, ALU.mult, ALU.add))
                did(dve.scalar_tensor_tensor(dst, z_sb[:, 2:SEQ + 2], conv_c[:, 2, c:c + 1], dst, ALU.mult, ALU.add))
                dve.tensor_tensor(dst, dst, gb_sb[:, :], ALU.mult).then_inc(conv_ready, 1)
                dve.wait_ge(conv_ready, c + 1)

            for s in range(3):
                for n in range(tiles_of[s]):
                    take(s, n)
                split_front(s + 2)
                if s == 0:
                    half = [w // 2 for w, _ in BRANCHES]
                    did(dve.tensor_scalar(seen[:, :], absd[:, :], float(half[0]), None, ALU.is_le))
                    did(dve.tensor_scalar(seen_b[:, :], step4[:, :], 0, None, ALU.is_equal))
                    did(dve.scalar_tensor_tensor(seen_b[:, :], absd[:, :], float(half[1]), seen_b[:, :],
                                                 ALU.is_le, ALU.mult))
                    did(dve.tensor_tensor(seen[:, :], seen[:, :], seen_b[:, :], ALU.add))
                    did(dve.tensor_scalar(seen_b[:, :], step16[:, :], 0, None, ALU.is_equal))
                    did(dve.scalar_tensor_tensor(seen_b[:, :], absd[:, :], float(half[2]), seen_b[:, :],
                                                 ALU.is_le, ALU.mult))
                    did(dve.tensor_tensor(seen[:, :], seen[:, :], seen_b[:, :], ALU.add))
                    inv = HEAD_DIM ** 0.5
                    did(dve.tensor_scalar(log_m[:, :], seen[:, :], 0.0, MASKED, ALU.is_equal, ALU.mult))
                    for m in range(2, len(BRANCHES) + 1):
                        did(dve.tensor_scalar(seen_b[:, :], seen[:, :], float(m), math.log(m) * inv,
                                              ALU.is_equal, ALU.mult))
                        did(dve.tensor_tensor(log_m[:, :], log_m[:, :], seen_b[:, :], ALU.add))

            dve.wait_ge(params_loaded, 16 * 9)
            for h in range(HEADS):
                s = 3 + h
                slope = 2.0 ** (-8.0 * (h + 1) / HEADS)
                did(dve.scalar_tensor_tensor(bias_h[:, :], absd[:, :], -slope * HEAD_DIM ** 0.5, log_m[:, :],
                                             ALU.mult, ALU.add))
                if h:
                    dve.wait_ge(probs_turned, h * TT)
                for t in range(TT):
                    dve.wait_ge(scores_ready, h * TT + t + 1)
                    shift = (TT - 1 - t) * P
                    dve.tensor_tensor_reduce(probs[:, t, :], bank[2 + t % 2][:, :], bias_h[:, shift:shift + SEQ],
                                             1.0, -3.0e38, ALU.add, ALU.max, max_s[:, h * TT + t:h * TT + t + 1])\
                       .then_inc(scores_taken, 1)
                dve.wait_ge(scores_taken, (h + 1) * TT)
                cols = slice(h * TT, (h + 1) * TT)
                dve.tensor_scalar(neg_max[:, cols], max_s[:, cols], -HEAD_DIM ** -0.5, None, ALU.mult)\
                   .then_inc(max_ready, 1)
                if h:
                    split_front(s + 1)
                dve.wait_ge(exp_ready, (h + 1) * TT)
                did(dve.reciprocal(rden[:, cols], den[:, cols]))
                for t in range(TT):
                    dve.tensor_scalar(probs[:, t, :], probs[:, t, :], rden[:, h * TT + t:h * TT + t + 1], None,
                                      ALU.mult).then_inc(probs_ready, 1)
                take(s, 0)
                take(s, 1)
                for c in range(TT):
                    dve.wait_ge(pT_hi_ready, h * TT + c + 1)
                    dve.tensor_tensor(pT_lo[:, c, :], bank[4 + c % 2][:, :], pT_hi[:, c, :], ALU.subtract)\
                       .then_inc(pT_lo_ready, 1)
            take(N_IN - 1, 0)
            split_front(N_IN)
            take(N_IN - 1, 1)

            def split_merged(k):
                dve.wait_ge(mT_hi_ready, k + 1)
                dve.scalar_tensor_tensor(mT_lo[:, k, :], merged[:, k, :], g_merge[:, k:k + 1], mT_hi[:, k, :],
                                         ALU.mult, ALU.subtract).then_inc(mT_lo_ready, 1)

            for k in range(NA):
                split_merged(k)
            split_front(N_IN + 1)
            for k in range(NA, KD):
                split_merged(k)
            dve.wait_ge(sq_attn_summed, NA)
            dve.wait_ge(sq_conv_summed, NC_)
            dve.tensor_reduce(ss_g, bank[7][:, 0:TT * KD].rearrange("p (t g k) -> p t g k", t=TT, g=2),
                                  AX.X, ALU.add).then_inc(sums_taken, 1)
            dve.wait_ge(sums_taken, 1)
            dve.tensor_scalar(std_g, ss_g, 1.0 / AW, EPS, ALU.mult, ALU.add).then_inc(var_g_ready, 1)
            dve.wait_ge(std_g_ready, 1)
            did(dve.reciprocal(rstd_g, std_g))
            split_front(N_IN + 2)
            dve.wait_ge(x_again, 16 * TT)
            for t in range(TT):
                for n in range(2):
                    dve.wait_ge(mix_ready, 2 * t + n + 1)
                    dst = x1[:, t, n * 512:(n + 1) * 512]
                    dve.scalar_tensor_tensor(dst, bank[2 * t + n][:, :], rstd_g[:, 2 * t:2 * t + 1], dst,
                                             ALU.mult, ALU.add).then_inc(mix_taken, 1)
            split_front(N_IN + 3)

            def take_x1T(t):
                dve.wait_ge(x1_turned, 2 * t + 2)
                dve.tensor_copy(x1T[:, TT:KD, t * P:(t + 1) * P],
                                bank[2 * t + 1][:, :].rearrange("p (k n) -> p k n", k=TT)).then_inc(x1T_dve_ready, 1)

            for t in range(TT):
                for n in range(2):
                    dve.wait_ge(mix_ready, 2 * TT + 2 * t + n + 1)
                    dve.wait_ge(mix_taken, 2 * TT)
                    dst = x1[:, t, n * 512:(n + 1) * 512]
                    dve.scalar_tensor_tensor(dst, bank[2 * t + n][:, :], rstd_g[:, 2 * t + 1:2 * t + 2], dst,
                                             ALU.mult, ALU.add).then_inc(mix_taken, 1)
                if t == 0:
                    for k in range(KD):
                        ins = dve.tensor_scalar(w_r[:, k, :], w_r[:, k, :], g_ffn[:, k:k + 1], None, ALU.mult)
                    ins.then_inc(w_r_ready, 1)
                else:
                    take_x1T(t - 1)
            take_x1T(TT - 1)
            dve.wait_ge(ss_1_ready, TT)
            dve.tensor_scalar(std_1, ss_1, 1.0 / D_MODEL, EPS, ALU.mult, ALU.add).then_inc(var_1_ready, 1)
            dve.wait_ge(std_1_ready, 1)
            dve.reciprocal(rstd_1, std_1).then_inc(rstd_1_ready, 1)
            dve.wait_ge(rstd_1_ready, 1)
            for t in range(TT):
                dve.wait_ge(router_ready, t + 1)
                ins = dve.scalar_tensor_tensor(logits[:, t, :], bank[2 * t][:, 0:E], rstd_1[:, t:t + 1], b_r[:, :],
                                               ALU.mult, ALU.add)
                did(ins)
            for t in range(TT):
                did(dve.max(top_v[:, t, :], logits[:, t, :]))
                did(dve.max_index(top_i[:, t, :], top_v[:, t, :], logits[:, t, :]))
            dve.tensor_tensor(gexp[:, :, :], top_v[:, :, 0:TOPK], top_v[:, :, 0:1].to_broadcast([P, TT, TOPK]),
                              ALU.subtract).then_inc(gate_shift_ready, 1)
            did(dve.tensor_copy(top_f[:, :, :], top_i[:, :, 0:TOPK]))
            dve.wait_ge(consts_made, 7)
            for t in range(TT):
                ins = dve.tensor_tensor(chosen[:, t, :, :], iota_e[:, :].unsqueeze(1).to_broadcast([P, TOPK, E]),
                                        top_f[:, t, :].unsqueeze(2).to_broadcast([P, TOPK, E]), ALU.is_equal)
                did(ins)
            for t in range(TT):
                dve.tensor_reduce(mask[:, t, :], chosen[:, t, :, :].rearrange("p k e -> p e k"), AX.X, ALU.add)\
                   .then_inc(mask_ready, 1)
            for t in range(2):
                dve.wait_ge(xn_scaled, t + 1)
                dve.tensor_tensor(xn[:, t, :], xn[:, t, :], g_ffn_row[:, :], ALU.mult).then_inc(xn_ready, 1)
            dve.wait_ge(rank_ready, 1)
            for t in range(TT):
                did(dve.tensor_tensor(rank[:, t, :], bank[1][:, t * E:(t + 1) * E], base_e[:, :], ALU.add))
            for t in range(TT):
                did(dve.tensor_tensor(chosen_p[:, t, :, :], chosen[:, t, :, :],
                                      rank[:, t, :].unsqueeze(1).to_broadcast([P, TOPK, E]), ALU.mult))
            did(dve.tensor_reduce(dest_f[:, :], chosen_p[:, :, :, :].rearrange("p t k e -> p (t k) e"), AX.X, ALU.add))
            did(dve.tensor_copy(dest[:, :], dest_f[:, :]))
            dve.wait_ge(gate_exp_ready, 1)
            did(dve.tensor_reduce(gsum[:, 0, :], gexp[:, :, :], AX.X, ALU.add))
            did(dve.reciprocal(gsum[:, 1, :], gsum[:, 0, :]))
            dve.wait_ge(entry_made, 1)
            for t in range(TT):
                ins = dve.tensor_scalar(entry[:, t * TOPK:(t + 1) * TOPK, 2].bitcast(F32), gexp[:, t, :],
                                        gsum[:, 1, t:t + 1], None, ALU.mult)
            ins.then_inc(entry_ready, 1)
            did(dve.tensor_reduce(cnt_f[:, 0:1], bank[3][:, 0:E], AX.X, ALU.max))
            did(dve.tensor_scalar(cnt_f[:, 1:2], cnt_f[:, 0:1], float(P), None, ALU.is_gt))
            for r in range(2, TT):
                did(dve.scalar_tensor_tensor(cnt_f[:, 1:2], cnt_f[:, 0:1], float(r * P), cnt_f[:, 1:2],
                                             ALU.is_gt, ALU.add))
            dve.tensor_copy(extra_sb[:, :], cnt_f[:, 1:2]).then_inc(extra_ready, 1)
            for t in range(2, TT):
                dve.wait_ge(xn_scaled, t + 1)
                dve.tensor_tensor(xn[:, t % 2, :], xn[:, t % 2, :], g_ffn_row[:, :], ALU.mult).then_inc(xn_ready, 1)
            dve.wait_ge(b_hi_ready, 1)
            dve.tensor_tensor(b_hl[E:2 * E, :], b_raw[E:2 * E, :], b_hl[E:2 * E, :], ALU.subtract).then_inc(b_ready, 1)

            def split(m, slot_no):
                dve.wait_ge(w_hi_ready, m + 1)
                if isinstance(m, int) and m < SPLIT:
                    wait_used(dve, N_FRONT - 1)
                else:
                    dve.wait_ge(w_used, m - (SPLIT - 1))
                dve.tensor_tensor(lo_slot(slot_no % SPLIT), raw_slot(slot_no % RAW), hi_slot(slot_no % SPLIT),
                                  ALU.subtract).then_inc(w_lo_ready, 1)

            def gu(j, i):
                split(gu_chunk(j, i), GU[i])

            def dn(j, i):
                split(dn_chunk(j, i), DN[i])

            def turned(j, hi, lo, hi_ready, lo_ready):
                for g in range(2):
                    dve.wait_ge(hi_ready, j * 2 + (g + 1))
                    rows = slice(g * TT, (g + 1) * TT)
                    dve.tensor_tensor(lo[:, rows, :].rearrange("p k n -> p (k n)"), bank[6 + g][:, :],
                                      hi[:, rows, :].rearrange("p k n -> p (k n)"), ALU.subtract).then_inc(lo_ready, 1)

            def clamp(j, used):
                dve.wait_ge(w_used, used)
                if not (isinstance(j, int) and j == 0):
                    dve.wait_ge(act_turned, j * 2)
                for n in range(2):
                    ins = dve.tensor_scalar(gate_in[:, n * 512:(n + 1) * 512], bank[n][:, :], LIMIT, None, ALU.min)
                ins.then_inc(gu_clamped, 1)
                for n in range(2):
                    ins = dve.tensor_scalar(lin_in[:, n * 512:(n + 1) * 512], bank[2 + n][:, :], LIMIT, -LIMIT,
                                            ALU.min, ALU.max)
                ins.then_inc(gu_clamped, 1)

            def gate(j):
                dve.wait_ge(gu_clamped, j * 2 + 2)
                dve.scalar_tensor_tensor(lin_in[:, :], lin_in[:, :], 1.0, gate_in[:, :], ALU.add, ALU.mult)\
                   .then_inc(lin_gated, 1)
                dve.wait_ge(lin_gated, j + 1)
                dve.wait_ge(sig_ready, j + 1)
                dve.tensor_tensor(lin_in[:, :], lin_in[:, :], sig_in[:, :], ALU.mult).then_inc(act_ready, 1)

            def select(dst, j, ready, used):
                column = sel_all[:, bass.ds(fixed(dve, expert(j)), 1)].to_broadcast([2 * E, P])
                if not (isinstance(j, int) and j == 0):
                    dve.wait_ge(used, j)
                dve.tensor_scalar(dst[:, :], column, 1.0, None, ALU.mult).then_inc(ready, 1)

            dve.wait_ge(pool_step, 6)
            select(sel_gu, 0, sel_gu_ready, sel_gu_used)
            for i in range(GU_CHUNKS):
                split(i, i)
                if i == 3:
                    select(sel_gu, 1, sel_gu_ready, sel_gu_used)
                if i == 1:
                    turned(0, xT_hi, xT_lo, xT_hi_ready, xT_lo_ready)
            clamp(0, GU_CHUNKS)

            def job(j, first=False):
                gu(j, 0)
                if first:
                    turned(1, xT_hi, xT_lo, xT_hi_ready, xT_lo_ready)
                gate(j - 1)
                for i in range(1, 4):
                    gu(j, i)
                select(sel_dn, j - 1, sel_dn_ready, sel_dn_used)
                select(sel_gu, j + 1, sel_gu_ready, sel_gu_used)
                for i in range(4, 7):
                    gu(j, i)
                turned(j - 1, aT_hi, aT_lo, aT_hi_ready, aT_lo_ready)
                gu(j, 7)
                dn(j - 1, 0)
                dn(j - 1, 1)
                clamp(j, gu_chunk(j, GU_CHUNKS - 1) + 1)
                dn(j - 1, 2)
                turned(j + 1, xT_hi, xT_lo, xT_hi_ready, xT_lo_ready)
                dn(j - 1, 3)

            job(1, first=True)
            end = jobs_end(dve)
            with dve.Fori(2, end) as j:
                job(j)
            last = end - 1
            select(sel_dn, last, sel_dn_ready, sel_dn_used)
            gate(last)
            split(last_dn_chunk(last, 0), DN_LAST[0])
            turned(last, aT_hi, aT_lo, aT_hi_ready, aT_lo_ready)
            for i in range(1, DN_CHUNKS):
                split(last_dn_chunk(last, i), DN_LAST[i])

            def scale(t):
                dve.wait_ge(ss_f_ready, t + 1)
                dve.tensor_scalar(std_f[:, t:t + 1], ss_f[:, t:t + 1], 1.0 / D_MODEL, EPS, ALU.mult, ALU.add)\
                   .then_inc(var_f_ready, 1)
                dve.wait_ge(std_f_ready, t + 1)
                dve.reciprocal(rstd_f[:, t:t + 1], std_f[:, t:t + 1]).then_inc(rstd_f_ready, 1)

            def gain(t):
                dve.wait_ge(out_scaled, t + 1)
                dve.tensor_tensor(x1[:, t, :], x1[:, t, :], g_fin_row[:, :], ALU.mult).then_inc(out_ready, 1)

            dve.wait_ge(g_fin_loaded, 16)
            for t in range(TT):
                dve.wait_ge(y_loaded[t % 2], 16 * (t // 2 + 1))
                for k in range(TOPK):
                    row = raw01[:, 2 * (t % 2) + k // 2, (k % 2) * D_MODEL:(k % 2 + 1) * D_MODEL]
                    ins = dve.tensor_tensor(x1[:, t, :], x1[:, t, :], row, ALU.add)
                    if k < TOPK - 1:
                        did(ins)
                ins.then_inc(y_added, 1)
                if t:
                    gain(t - 1)
                scale(t)
            gain(TT - 1)

        @block.tensor
        def _(pe):
            def product(dst, a_hi, a_lo, b_hi, b_lo, start, stop):
                pe.matmul(dst, a_hi, b_hi, start=start, stop=False)
                pe.matmul(dst, a_hi, b_lo, start=False, stop=False)
                return pe.matmul(dst, a_lo, b_hi, start=False, stop=stop)

            pe.wait_ge(consts_made, 2)
            for t in range(TT):
                pe.wait_ge(x_scaled_ready, t + 1)
                for k in range(KD):
                    ins = pe.transpose(bank[k][:, t * P:(t + 1) * P], x_scaled[:, t, k * P:(k + 1) * P], ident[:, :])
                    if t == TT - 1:
                        ins.then_inc(xT_turned, 1)
            pe.wait_ge(xnT_lo_ready, KD)

            def project(s, n):
                i = first_tile[s] + n
                if n == 0:
                    pe.wait_ge(front_lo, s + 1)
                if i >= 2:
                    pe.wait_ge(proj_taken, i - 1)
                hi = hi01[:, s % 2, :].rearrange("p (k n) -> p k n", k=KD)
                lo = lo01[:, s % 2, :].rearrange("p (k n) -> p k n", k=KD)
                for k in range(KD):
                    if chunks[s][0] == "v":
                        cols = slice(n * P, (n + 1) * P)
                        ins = product(bank[i % 2][:, 0:2 * P], xnT_hi[:, k, cols], xnT_lo[:, k, cols],
                                      hi[:, k, :], lo[:, k, :], k == 0, k == KD - 1)
                    else:
                        cols = slice(n * P, (n + 1) * P)
                        ins = product(bank[i % 2][:, :], hi[:, k, cols], lo[:, k, cols],
                                      xnT_hi[:, k, :], xnT_lo[:, k, :], k == 0, k == KD - 1)
                ins.then_inc(proj_ready, 1)

            for s in range(3):
                for n in range(tiles_of[s]):
                    project(s, n)

            def attend(h):
                pair = slice(h // 2 * P, h // 2 * P + P)
                if h:
                    pe.wait_ge(heads_taken, h)
                for c in range(TT):
                    pe.wait_ge(pT_lo_ready, h * TT + c + 1)
                    ins = product(bank[6][:, :], v_hi[:, c, pair], v_lo[:, c, pair], pT_hi[:, c, :], pT_lo[:, c, :],
                                  c == 0, c == TT - 1)
                ins.then_inc(heads_ready, 1)

            def sum_squares(k, ready, number, summed):
                pe.wait_ge(ready, number)
                for t in range(TT):
                    ins = pe.matmul(bank[7][:, t * KD + k:t * KD + k + 1],
                                    sq_sb[:, 0 if k < NA else 1, t * P:(t + 1) * P], ones[:, 0:1], start=True, stop=True)
                ins.then_inc(summed, 1)

            pe.wait_ge(consts_made, 3)
            for h in range(HEADS):
                s = 3 + h
                rows, pair = slice(HEAD_DIM * (h % 2), HEAD_DIM * (h % 2) + HEAD_DIM), h // 2 % 2
                pe.wait_ge(proj_taken, first_tile[[0, 3, 5, 7][h // 2]] + 2)
                for t in range(TT):
                    n = h * TT + t
                    if n >= 2:
                        pe.wait_ge(scores_taken, n - 1)
                    q = slice(t * P, (t + 1) * P)
                    product(bank[2 + t % 2][:, :], qk_hi[rows, pair, 0, q], qk_lo[rows, pair, 0, q],
                            qk_hi[rows, pair, 1, :], qk_lo[rows, pair, 1, :], True, True).then_inc(scores_ready, 1)
                project(s, 0)
                if h:
                    attend(h - 1)
                project(s, 1)
                pe.wait_ge(probs_ready, (h + 1) * TT)
                for c in range(TT):
                    if h * TT + c >= 2:
                        pe.wait_ge(pT_lo_ready, h * TT + c - 1)
                    for t in range(TT):
                        ins = pe.transpose(bank[4 + c % 2][:, t * P:(t + 1) * P], probs[:, t, c * P:(c + 1) * P],
                                           ident[:, :])
                    ins.then_inc(probs_turned, 1)
                if h in (3, 5, 7):
                    pair_no = (h - 3) // 2
                    sum_squares(pair_no, sq_attn_ready, pair_no + 1, sq_attn_summed)
                if h in (5, 7):
                    c = (h - 5) // 2
                    sum_squares(NA + c, sq_conv_ready, c + 1, sq_conv_summed)
            project(N_IN - 1, 0)
            attend(HEADS - 1)
            project(N_IN - 1, 1)
            sum_squares(NA - 1, sq_attn_ready, NA, sq_attn_summed)

            for half in range(2):
                if half == 0:
                    pe.wait_ge(proj_taken, first_tile[N_IN])
                    pe.wait_ge(heads_taken, HEADS)
                for c in range(2):
                    s = N_IN + 2 * half + c
                    if s == N_IN:
                        sum_squares(NA + 2, sq_conv_ready, 3, sq_conv_summed)
                    pe.wait_ge(front_lo, s + 1)
                    pe.wait_ge(mT_lo_ready, 4 * half + 2 * c + 2)
                    for t in range(TT):
                        for n in range(2):
                            b = 2 * t + n
                            if s == N_IN and b == 6:
                                sum_squares(NA + 3, sq_conv_ready, NC_, sq_conv_summed)
                            if s == N_IN and b == 7:
                                pe.wait_ge(sums_taken, 1)
                            if half == 1 and c == 0:
                                pe.wait_ge(mix_taken, b + 1)
                            for i in range(2):
                                k, q, cols = 4 * half + 2 * c + i, slice(t * P, (t + 1) * P), \
                                    slice(i * D_MODEL + n * 512, i * D_MODEL + (n + 1) * 512)
                                ins = product(bank[b][:, :], mT_hi[:, k, q], mT_lo[:, k, q], hi01[:, s % 2, cols],
                                              lo01[:, s % 2, cols], c == 0 and i == 0, c == 1 and i == 1)
                            if c == 1:
                                ins.then_inc(mix_ready, 1)
                    if c == 0:
                        ins.then_inc(mix_half_used, 1)

            pe.wait_ge(w_r_ready, 1)
            for t in range(TT):
                pe.wait_ge(mix_taken, 2 * TT + 2 * t + 2)
                for g in range(2):
                    for k in range(TT):
                        ins = pe.transpose(bank[2 * t + g][:, k * P:(k + 1) * P],
                                           x1[:, t, (g * TT + k) * P:(g * TT + k + 1) * P], ident[:, :])
                    ins.then_inc(x1_turned, 1)
            for t in range(TT):
                pe.wait_ge(x1T_act_ready, t + 1)
                pe.wait_ge(x1T_dve_ready, t + 1)
                for k in range(KD):
                    ins = pe.matmul(bank[2 * t][:, 0:E], x1T[:, k, t * P:(t + 1) * P], w_r[:, k, :],
                                    start=k == 0, stop=k == KD - 1)
                ins.then_inc(router_ready, 1)
            pe.wait_ge(consts_made, 7)
            for t in range(TT):
                pe.wait_ge(mask_ready, t + 1)
                for u in range(t + 1):
                    pe.matmul(bank[1][:, t * E:(t + 1) * E], before[:, :] if u == t else ones[:, :], mask[:, u, :],
                              start=u == 0, stop=u == t)
            for u in range(TT):
                ins = pe.matmul(bank[3][:, 0:E], ones[:, :], mask[:, u, :], start=u == 0, stop=u == TT - 1)
            ins.then_inc(rank_ready, 1)

            def transpose_got(j):
                pe.wait_ge(x_gathered, j * 16 + 16)
                turn(x_got, got_turned)

            def turn(src, done):
                for g in range(2):
                    for k in range(TT):
                        ins = pe.transpose(bank[6 + g][:, k * P:(k + 1) * P],
                                           src[:, (g * TT + k) * P:(g * TT + k + 1) * P], ident[:, :])
                    ins.then_inc(done, 1)

            def turn_act(j):
                pe.wait_ge(act_ready, j + 1)
                turn(lin_in, act_turned)

            def bias_gu(j):
                pe.wait_ge(sel_gu_ready, j + 1)
                for n in range(4):
                    ins = pe.matmul(bank[n][:, :], sel_gu[:, :], b_hl[:, n * 512:(n + 1) * 512], start=True, stop=False)
                ins.then_inc(sel_gu_used, 1)

            def gate_up(m, slot_no, i):
                pe.wait_ge(w_lo_ready, m + 1)
                hi, lo = hi_slot(slot_no % SPLIT), lo_slot(slot_no % SPLIT)
                last = i == GU_CHUNKS - 1
                for a, w, end_ in ((xT_hi, hi, False), (xT_hi, lo, False), (xT_lo, hi, last)):
                    for n in range(4):
                        ins = pe.matmul(bank[n][:, :], a[:, i, :], w[:, n * 512:(n + 1) * 512], start=False, stop=end_)
                ins.then_inc(w_used, 1)

            def bias_dn(j):
                pe.wait_ge(y_ready, j)
                pe.wait_ge(sel_dn_ready, j + 1)
                for n in range(2):
                    ins = pe.matmul(bank[4 + n][:, :], sel_dn[:, :], b_hl[:, (4 + n) * 512:(5 + n) * 512],
                                    start=True, stop=False)
                ins.then_inc(sel_dn_used, 1)

            def down(m, slot_no, i):
                pe.wait_ge(w_lo_ready, m + 1)
                hi, lo = hi_slot(slot_no % SPLIT), lo_slot(slot_no % SPLIT)
                for r in range(2):
                    last = i == DN_CHUNKS - 1 and r == 1
                    for a, w, end_ in ((aT_hi, hi, False), (aT_hi, lo, False), (aT_lo, hi, last)):
                        for n in range(2):
                            ins = pe.matmul(bank[4 + n][:, :], a[:, 2 * i + r, :],
                                            w[:, r * D_MODEL + n * 512:r * D_MODEL + (n + 1) * 512],
                                            start=False, stop=end_)
                ins.then_inc(w_used, 1)

            pe.wait_ge(extra_ready, 1)
            transpose_got(0)
            pe.wait_ge(b_ready, 1)
            bias_gu(0)
            pe.wait_ge(xT_lo_ready, 2)
            for i in range(GU_CHUNKS):
                gate_up(i, GU0[i], i)
            transpose_got(1)

            def job(j):
                pe.wait_ge(gu_clamped, j * 2)
                bias_gu(j)
                pe.wait_ge(xT_lo_ready, j * 2 + 2)
                for i in range(GU_CHUNKS):
                    gate_up(gu_chunk(j, i), GU[i], i)
                    if i == 3:
                        turn_act(j - 1)
                pe.wait_ge(aT_lo_ready, j * 2)
                transpose_got(j + 1)
                bias_dn(j - 1)
                for i in range(DN_CHUNKS):
                    down(dn_chunk(j - 1, i), DN[i], i)

            job(1)
            end = jobs_end(pe)
            with pe.Fori(2, end) as j:
                job(j)
            last = end - 1
            pe.wait_ge(xT_lo_ready, end * 2 + 2)
            turn_act(last)
            bias_dn(last)
            pe.wait_ge(aT_lo_ready, end * 2)
            for i in range(DN_CHUNKS):
                down(last_dn_chunk(last, i), DN_LAST[i], i)


_INS = ['x', 'mix_norm_g', 'w_in', 'conv_w', 'attn_out_norm_g', 'conv_out_norm_g', 'w_out', 'ffn_norm_g',
        'w_router', 'b_router', 'w_gate_up', 'b_gate_up', 'w_down', 'b_down', 'final_norm_g']
_OUTS = [((1, SEQ, D_MODEL), 'float32')]


def kernel(**inputs):
    import numpy as _np
    import concourse.bacc as _bacc
    from concourse import mybir as _mybir
    from concourse.bass_utils import run_bass_kernel_spmd as _run

    nc = _bacc.Bacc("TRN2", target_bir_lowering=False, num_devices=1)
    arrays, args = {}, []
    for name in _INS:
        a = _np.ascontiguousarray(inputs[name])
        arrays[f"in_{name}_dram"] = a
        args.append(nc.dram_tensor(f"in_{name}_dram", a.shape, _mybir.dt.from_np(a.dtype), kind="ExternalInput").ap())
    for i, (shape, dtype) in enumerate(_OUTS):
        dt = _mybir.dt.from_np(_np.dtype(dtype))
        args.append(nc.dram_tensor(f"out_{i}_dram", shape, dt, kind="ExternalOutput").ap())
    build(nc, *args)
    r = _run(nc, [arrays], core_ids=[0])
    return r.results[0]["out_0_dram"]
```

```python
from contextlib import ExitStack
import math

import concourse.bass as bass
from concourse import mybir

P = 128
F32 = mybir.dt.float32
F32R = mybir.dt.float32r
I32 = mybir.dt.int32
U32 = mybir.dt.uint32
ALU = mybir.AluOpType
ACT = mybir.ActivationFunctionType
AX = mybir.AxisListType

SEQ, D_MODEL = 512, 1024
TT = SEQ // P
KD = D_MODEL // P
HEADS, HEAD_DIM = 8, 64
AW = HEADS * HEAD_DIM
CW = D_MODEL - AW
NA, NC_ = AW // P, CW // P
BRANCHES = ((128, 1), (512, 4), (2048, 16))
E, TOPK = 32, 4
D_FF = D_MODEL
EPS = 1e-5
LIMIT, ALPHA = 7.0, 1.702
CHUNK = 2048
RAW_FRONT, SPLIT_FRONT = 4, 2
RAW, SPLIT = 12, 3
GU_CHUNKS = D_MODEL // P
DN_CHUNKS = D_FF // (2 * P)
JOB = GU_CHUNKS + DN_CHUNKS
IN_FLIGHT = 3
TILE = 96
ROUNDS = -(-SEQ // TILE)
LIST = ROUNDS * TILE
ROWS = E * LIST
NONE = 65535
MASKED = -1e30


def front_chunks():
    q, k, v, gb, gc, u = (AW // P * i for i in range(6))
    qk = [("qk", q + p, k + p) for p in range(NA)]
    conv = [("conv", gb, gc), ("conv", u, u + 1), ("conv", gb + 1, gc + 1),
            ("conv", u + 2, u + 3), ("conv", gb + 2, gc + 2), ("conv", gb + 3, gc + 3)]
    return [qk[0], ("v", v, v + 1), ("v", v + 2, v + 3), qk[1], conv[0], qk[2], conv[1], qk[3],
            conv[2], conv[3], conv[4], conv[5]]


CONV_TILES = [("gb", 0), ("gc", 0), ("u", 0), ("u", 1), ("gb", 1), ("gc", 1),
              ("u", 2), ("u", 3), ("gb", 2), ("gc", 2), ("gb", 3), ("gc", 3)]
CONV_DONE = [2, 5, 9, 11]


def build(nc, x, mix_norm_g, w_in, conv_w, attn_out_norm_g, conv_out_norm_g, w_out, ffn_norm_g,
          w_router, b_router, w_gate_up, b_gate_up, w_down, b_down, final_norm_g, out):
    chunks = front_chunks()
    N_IN = len(chunks)
    N_FRONT = N_IN + D_MODEL // (2 * P)
    tiles_of = [TT if c[0] == "v" else 2 for c in chunks]
    first_tile = [sum(tiles_of[:i]) for i in range(N_IN + 1)]

    xn_rows = nc.dram_tensor("xn_rows", (SEQ, D_MODEL), F32, kind="Internal").ap()
    lists = nc.dram_tensor("lists", (ROWS, 4), U32, kind="Internal").ap()
    sum_rows = nc.dram_tensor("sum_rows", (SEQ, D_MODEL), F32, kind="Internal").ap()

    ctx = ExitStack()

    def sb(name, shape, dt=F32):
        return ctx.enter_context(nc.sbuf_tensor(name, shape, dt))

    def sem(name):
        return ctx.enter_context(nc.semaphore(name))

    def overlay(offset, *tensors):
        with ExitStack() as c:
            if offset:
                c.enter_context(nc.sbuf_tensor(f"before_{tensors[0][0]}", [P, offset // 4], F32))
            got = [c.enter_context(nc.sbuf_tensor(n, s, d)) for n, s, d in tensors]
        return got if len(got) > 1 else got[0]

    with ctx:
        raw01 = sb("raw01", [P, RAW_FRONT, CHUNK])
        hi01 = sb("hi01", [P, SPLIT_FRONT, CHUNK], F32R)
        lo01 = sb("lo01", [P, SPLIT_FRONT, CHUNK], F32R)
        ident = sb("ident", [P, P])
        g_mix = sb("g_mix", [P, KD])
        g_merge = sb("g_merge", [P, KD])
        g_ffn = sb("g_ffn", [P, KD])
        conv_c = sb("conv_c", [P, 3, NC_])
        stats = sb("stats", [P, 64])
        ss_x, std_x, rstd_x = (stats[:, TT * i:TT * i + TT] for i in range(3))
        ss_g, std_g, rstd_g = (stats[:, 16 + 8 * i:24 + 8 * i] for i in range(3))
        ss_1, std_1, rstd_1 = (stats[:, 40 + TT * i:44 + TT * i] for i in range(3))
        ss_f, std_f, rstd_f = (stats[:, 52 + TT * i:56 + TT * i] for i in range(3))
        max_s = sb("max_s", [P, HEADS * TT])
        neg_max = sb("neg_max", [P, HEADS * TT])
        den = sb("den", [P, HEADS * TT])
        rden = sb("rden", [P, HEADS * TT])
        ones = sb("ones", [P, P])
        sel_all = sb("sel_all", [2 * E, E])
        sel_gu = sb("sel_gu", [2 * E, TILE], F32R)
        sel_dn = sb("sel_dn", [2 * E, TILE], F32R)
        gather_list = sb("gather_list", [P, 4], U32)
        scatter_list = sb("scatter_list", [P, 4], U32)
        extra_sb = sb("extra_sb", [P, 1], I32)
        g_ffn_row = sb("g_ffn_row", [P, D_MODEL])
        w_r = sb("w_r", [P, KD, E])
        b_r = sb("b_r", [P, E])

        K, W = 1024, 896
        merged = overlay(0, ("merged", [P, KD, SEQ], F32))
        sq_x, diag = overlay(0, ("sq_x", [P, D_MODEL], F32), ("diag", [P, TT, P], F32))
        xnT_hi, xnT_lo = overlay(16 * K, ("xnT_hi", [P, KD, SEQ], F32R), ("xnT_lo", [P, KD, SEQ], F32R))
        qk_hi, qk_lo = overlay(48 * K, ("qk_hi", [P, 2, 2, SEQ], F32R), ("qk_lo", [P, 2, 2, SEQ], F32R))
        v_hi, v_lo = overlay(64 * K, ("v_hi", [P, TT, AW], F32R), ("v_lo", [P, TT, AW], F32R))
        x_sb = overlay(64 * K, ("x_sb", [P, TT, D_MODEL], F32))
        probs, pT_hi, pT_lo = overlay(80 * K, ("probs", [P, TT, SEQ], F32), ("pT_hi", [P, TT, SEQ], F32R),
                                      ("pT_lo", [P, TT, SEQ], F32R))
        diff, step4, step16, seen, seen_b, seen_c = overlay(
            80 * K, ("diff", [P, W], I32), ("step4", [P, W], I32), ("step16", [P, W], I32),
            ("seen", [P, W], F32), ("seen_b", [P, W], F32), ("seen_c", [P, W], F32))
        absd, log_m, bias_h, gb_sb, gc_sb, u_sb, z_sb, sq_sb, tap = overlay(
            104 * K, ("absd", [P, W], F32), ("log_m", [P, W], F32), ("bias_h", [P, 2, W], F32),
            ("gb_sb", [P, SEQ], F32), ("gc_sb", [P, SEQ], F32), ("u_sb", [P, 2, SEQ], F32),
            ("z_sb", [P, SEQ + 2], F32), ("sq_sb", [P, 2, SEQ], F32), ("tap", [P, SEQ], F32))
        mT_hi, mT_lo = overlay(16 * K, ("mT_hi", [P, KD, SEQ], F32R), ("mT_lo", [P, KD, SEQ], F32R))
        x1 = overlay(48 * K, ("x1", [P, TT, D_MODEL], F32))
        x1T = overlay(64 * K, ("x1T", [P, KD, SEQ], F32))
        xn = x1
        b_raw_gu = overlay(80 * K, ("b_raw_gu", [2 * E, 2 * D_FF], F32))
        sq_x1, b_raw_dn = overlay(126 * K, ("sq_x1", [P, D_MODEL], F32), ("b_raw_dn", [2 * E, D_FF], F32))
        pick_1, chosen_p = overlay(64 * K, ("pick_1", [P, TT, TILE], F32), ("chosen_p", [P, TT, TOPK, E], F32))
        pick, iota_n = overlay(28 * K, ("pick", [P, TT, TILE], F32), ("iota_n", [P, TILE], F32))
        empty = overlay(88 * K, ("empty", [P, ROWS // P * 4], U32))
        (logits, top_v, top_i, top_f, gexp, gsum, chosen, mask, rank, dest_f, dest, entry,
         iota_e, base_e, before, cnt_f, token, token_1) = overlay(
            92 * K, ("logits", [P, TT, E], F32), ("top_v", [P, TT, 8], F32), ("top_i", [P, TT, 8], U32),
            ("top_f", [P, TT, TOPK], F32), ("gexp", [P, TT, TOPK], F32), ("gsum", [P, 2, TT], F32),
            ("chosen", [P, TT, TOPK, E], F32), ("mask", [P, TT, E], F32), ("rank", [P, TT, E], F32),
            ("dest_f", [P, TT * TOPK], F32), ("dest", [P, TT * TOPK], U32),
            ("entry", [P, TT * TOPK, 4], U32), ("iota_e", [P, E], F32), ("base_e", [P, E], F32),
            ("before", [P, P], F32), ("cnt_f", [P, 4], F32),
            ("token", [P, TT], F32), ("token_1", [P, TT], F32))
        raw_b = overlay(32 * K, ("raw_b", [P, 2, CHUNK], F32))
        hi2, lo2 = overlay(0, ("hi2", [P, CHUNK], F32R), ("lo2", [P, CHUNK], F32R))
        xT_hi, xT_lo, x_got, aT_lo = overlay(
            16 * K, ("xT_hi", [P, KD, TILE], F32R), ("xT_lo", [P, KD, TILE], F32R),
            ("x_got", [P, D_MODEL], F32), ("aT_lo", [P, KD, TILE], F32R))
        gate_in, lin_in, sig_in, aT_hi = overlay(
            48 * K, ("gate_in", [P, D_FF], F32), ("lin_in", [P, D_FF], F32), ("sig_in", [P, D_FF], F32),
            ("aT_hi", [P, KD, TILE], F32R))
        y_out, raw_c, raw_d = overlay(64 * K, ("y_out", [P, D_MODEL], F32), ("raw_c", [P, 2, CHUNK], F32),
                                      ("raw_d", [P, 1, CHUNK], F32))
        b_hl, raw_a, raw_e = overlay(98 * K, ("b_hl", [2 * E, 3 * D_FF], F32R), ("raw_a", [P, 2, CHUNK], F32),
                                     ("raw_e", [P, 1, CHUNK], F32))
        g_fin_row = overlay(92 * K, ("g_fin_row", [P, D_MODEL], F32))

        bank = [ctx.enter_context(nc.psum_tensor(f"bank{i}", [P, 512], F32)) for i in range(8)]

        x_loaded = [sem(f"x_loaded{t}") for t in range(TT)]
        x_again = sem("x_again")
        params_loaded = sem("params_loaded")
        g_mix_loaded = sem("g_mix_loaded")
        front_loaded = [sem(f"front_loaded{i}") for i in range(RAW_FRONT)]
        consts_made, sel_all_made = sem("consts_made"), sem("sel_all_made")
        bits_ready, bias_ready = sem("bits_ready"), sem("bias_ready")
        pool_step, dve_step = sem("pool_step"), sem("dve_step")
        ss_x_ready, var_x_ready, std_x_ready = sem("ss_x_ready"), sem("var_x_ready"), sem("std_x_ready")
        rstd_x_ready, diag_ready = sem("rstd_x_ready"), sem("diag_ready")
        xT_turned, xnT_hi_ready, xnT_lo_ready = sem("xT_turned"), sem("xnT_hi_ready"), sem("xnT_lo_ready")
        front_hi, front_lo, mix_half_used = sem("front_hi"), sem("front_lo"), sem("mix_half_used")
        sums_taken = sem("sums_taken")
        proj_ready, proj_hi_ready, proj_taken = sem("proj_ready"), sem("proj_hi_ready"), sem("proj_taken")
        scores_ready, scores_taken = sem("scores_ready"), sem("scores_taken")
        max_ready, exp_ready, probs_ready = sem("max_ready"), sem("exp_ready"), sem("probs_ready")
        probs_turned, pT_hi_ready, pT_lo_ready = sem("probs_turned"), sem("pT_hi_ready"), sem("pT_lo_ready")
        heads_ready, heads_taken = sem("heads_ready"), sem("heads_taken")
        sq_attn_ready, sq_attn_summed = sem("sq_attn_ready"), sem("sq_attn_summed")
        conv_ready = sem("conv_ready")
        sq_conv_ready, sq_conv_summed = sem("sq_conv_ready"), sem("sq_conv_summed")
        var_g_ready, std_g_ready = sem("var_g_ready"), sem("std_g_ready")
        mT_hi_ready, mT_lo_ready = sem("mT_hi_ready"), sem("mT_lo_ready")
        mix_ready, mix_taken = sem("mix_ready"), sem("mix_taken")
        x1_turned, x1T_act_ready, x1T_dve_ready = sem("x1_turned"), sem("x1T_act_ready"), sem("x1T_dve_ready")
        router_ready = sem("router_ready")
        ss_1_ready, var_1_ready, std_1_ready, rstd_1_ready = (
            sem("ss_1_ready"), sem("var_1_ready"), sem("std_1_ready"), sem("rstd_1_ready"))
        xn_scaled, xn_dve_ready, xn_pool_ready, xn_stored = (
            sem("xn_scaled"), sem("xn_dve_ready"), sem("xn_pool_ready"), sem("xn_stored"))
        w_r_ready, x1_stored = sem("w_r_ready"), sem("x1_stored")
        gate_shift_ready, gate_exp_ready = sem("gate_shift_ready"), sem("gate_exp_ready")
        mask_ready, rank_ready, counts_ready = sem("mask_ready"), sem("rank_ready"), sem("counts_ready")
        iota_n_made, pick_ready = sem("iota_n_made"), sem("pick_ready")
        pick_1_ready, places_1_ready, list_1_ready = sem("pick_1_ready"), sem("places_1_ready"), sem("list_1_ready")
        entry_made, entry_ready = sem("entry_made"), sem("entry_ready")
        extra_ready = sem("extra_ready")
        lists_emptied, lists_ready = sem("lists_emptied"), sem("lists_ready")
        b_loaded, b_hi_ready, b_ready = sem("b_loaded"), sem("b_hi_ready"), sem("b_ready")
        w_loaded = [sem(f"w_loaded{i}") for i in range(RAW)]
        w_hi_ready, w_lo_ready, w_used = sem("w_hi_ready"), sem("w_lo_ready"), sem("w_used")
        gather_list_loaded, x_gathered = sem("gather_list_loaded"), sem("x_gathered")
        x_got_cleared = sem("x_got_cleared")
        got_turned, xT_hi_ready, xT_lo_ready = sem("got_turned"), sem("xT_hi_ready"), sem("xT_lo_ready")
        sel_gu_ready, sel_gu_used = sem("sel_gu_ready"), sem("sel_gu_used")
        sel_dn_ready, sel_dn_used = sem("sel_dn_ready"), sem("sel_dn_used")
        gu_clamped, sig_ready = sem("gu_clamped"), sem("sig_ready")
        lin_gated, act_ready = sem("lin_gated"), sem("act_ready")
        act_turned, aT_hi_ready, aT_lo_ready = sem("act_turned"), sem("aT_hi_ready"), sem("aT_lo_ready")
        y_half_ready, y_ready = sem("y_half_ready"), sem("y_ready")
        scatter_list_loaded, y_stored = sem("scatter_list_loaded"), sem("y_stored")
        g_fin_loaded = sem("g_fin_loaded")
        sum_loaded = [sem(f"sum_loaded{t}") for t in range(TT)]
        ss_f_ready, var_f_ready, std_f_ready = sem("ss_f_ready"), sem("var_f_ready"), sem("std_f_ready")
        rstd_f_ready, out_ready, out_stored = sem("rstd_f_ready"), sem("out_ready"), sem("out_stored")

        def raw_slot(m):
            for ring in (raw01, raw_a, raw_d, raw_b, raw_e, raw_c):
                if m < ring.shape[1]:
                    return ring[:, m, :]
                m -= ring.shape[1]

        def hi_slot(m):
            return [hi2[:, :], hi01[:, 0, :], hi01[:, 1, :]][m]

        def lo_slot(m):
            return [lo2[:, :], lo01[:, 0, :], lo01[:, 1, :]][m]

        def gu_chunk(j, i):
            return i if isinstance(j, int) and j == 0 else (j - 1) * JOB + (GU_CHUNKS + i)

        def dn_chunk(j, i):
            return j * JOB + (2 * GU_CHUNKS + i)

        def last_dn_chunk(j, i):
            return (j * JOB) + (GU_CHUNKS + i)

        GU0 = [i for i in range(GU_CHUNKS)]
        GU = [GU_CHUNKS + i for i in range(GU_CHUNKS)]
        DN = [2 * GU_CHUNKS + i for i in range(DN_CHUNKS)]
        DN_LAST = [GU_CHUNKS + i for i in range(DN_CHUNKS)]
        assert JOB == RAW and JOB % SPLIT == 0

        def expert(j):
            return j % E if isinstance(j, int) else j & (E - 1)

        def round_(j):
            return j // E if isinstance(j, int) else j >> (E.bit_length() - 1)

        def fixed(eng, value):
            return value if isinstance(value, int) else eng.snap(eng.to_reg(value))

        def is_split(i):
            return next(c[0] for n, c in enumerate(chunks) if i < first_tile[n + 1]) != "conv"

        def conv_tile(c):
            return [i for i in range(first_tile[N_IN]) if not is_split(i)][c]

        def splits_to(i):
            return sum(is_split(n) for n in range(i + 1))

        def jobs_end(eng):
            eng.wait_ge(extra_ready, 1)
            extra = eng.value_load(extra_sb[0:1, 0:1], min_val=0, max_val=ROUNDS - 1)
            return eng.snap(extra * E + E)

        def wait_used(eng, s):
            if s < N_IN:
                eng.wait_ge(proj_ready, first_tile[s + 1])
            elif (s - N_IN) % 2 == 0:
                eng.wait_ge(mix_half_used, (s - N_IN) // 2 + 1)
            else:
                eng.wait_ge(mix_ready, 2 * TT * ((s - N_IN) // 2 + 1))

        def wait_split_slot(eng, m):
            if m == 0:
                eng.wait_ge(mT_hi_ready, KD)
                eng.wait_ge(mT_lo_ready, KD)
                eng.wait_ge(sq_conv_ready, NC_)
            else:
                wait_used(eng, N_FRONT - SPLIT_FRONT + m - 1)

        block = ctx.enter_context(nc.Block())

        @block.sync
        def _(sp):
            for t in range(TT):
                sp.dma_start(x_sb[:, t, :], x[0, t * P:(t + 1) * P, :]).then_inc(x_loaded[t], 16)
            w_in_v = w_in[0].rearrange("(k p) n -> p k n", p=P)
            for s in range(N_FRONT):
                if s >= RAW_FRONT:
                    sp.wait_ge(front_hi, s - RAW_FRONT + 1)
                    sp.wait_ge(front_lo, s - RAW_FRONT + 1)
                slot = raw01[:, s % RAW_FRONT, :]
                for n in range(2):
                    if s < N_IN:
                        c = chunks[s][1 + n]
                        src = w_in_v[:, :, c * P:(c + 1) * P]
                        dst = slot.rearrange("p (k two n) -> p k two n", k=KD, two=2)[:, :, n, :]
                    else:
                        c = 2 * (s - N_IN) + n
                        src, dst = w_out[0, c * P:(c + 1) * P, :], slot[:, n * D_MODEL:(n + 1) * D_MODEL]
                    sp.dma_start(dst, src).then_inc(front_loaded[s % RAW_FRONT], 16)

            def load_gu(e, i, m, slot_no, loads):
                wait_slot(m, slot_no, loads)
                sp.dma_start(raw_slot(slot_no % RAW), w_gate_up[0, e, i * P:(i + 1) * P, :])\
                  .then_inc(w_loaded[slot_no % RAW], 16)

            def load_dn(e, i, m, slot_no, loads):
                wait_slot(m, slot_no, loads)
                sp.dma_start(raw_slot(slot_no % RAW).rearrange("p (i n) -> p i n", i=2),
                             w_down[0, e, 2 * i * P:2 * (i + 1) * P, :].rearrange("(i p) n -> p i n", p=P))\
                  .then_inc(w_loaded[slot_no % RAW], 16)

            def wait_slot(m, slot_no, loads):
                if not isinstance(m, int) or m >= RAW:
                    split_ = fixed(sp, m - (RAW - 1))
                    sp.wait_ge(w_loaded[(slot_no - IN_FLIGHT) % RAW], loads[(slot_no - IN_FLIGHT) // RAW])
                    sp.wait_ge(w_hi_ready, split_)
                    sp.wait_ge(w_lo_ready, split_)
                    return
                if m >= IN_FLIGHT:
                    sp.wait_ge(w_loaded[m - IN_FLIGHT], 16)
                if m < RAW_FRONT:
                    s = N_IN + m
                    sp.wait_ge(front_hi, s + 1)
                    sp.wait_ge(front_lo, s + 1)
                elif m == RAW_FRONT:
                    sp.wait_ge(conv_ready, NC_)
                    sp.wait_ge(sq_attn_summed, NA)
                    sp.wait_ge(sq_conv_summed, NC_)
                    sp.wait_ge(scores_taken, HEADS * TT)
                elif m == RAW_FRONT + 2:
                    sp.wait_ge(lists_emptied, 16)
                    sp.wait_ge(b_ready, 1)
                elif m == RAW_FRONT + 3:
                    wait_used(sp, N_FRONT - 1)
                elif m == RAW_FRONT + 5:
                    sp.wait_ge(ss_1_ready, TT)
                elif m == RAW_FRONT + 6:
                    sp.wait_ge(router_ready, TT)

            def load_counts(j):
                return fixed(sp, j * 16), fixed(sp, j * 16 + 16)

            def job(j):
                e, before_e = fixed(sp, expert(j)), fixed(sp, expert(j - 1))
                loads = load_counts(j)
                for i in range(GU_CHUNKS):
                    load_gu(e, i, gu_chunk(j, i), GU[i], loads)
                for i in range(DN_CHUNKS):
                    load_dn(before_e, i, dn_chunk(j - 1, i), DN[i], loads)

            for i in range(GU_CHUNKS):
                load_gu(0, i, i, GU0[i], None)
            job(1)
            end = jobs_end(sp)
            with sp.Fori(2, end) as j:
                job(j)
            loads = load_counts(end)
            for i in range(DN_CHUNKS):
                load_dn(E - 1, i, last_dn_chunk(end - 1, i), DN_LAST[i], loads)

            sp.wait_ge(extra_ready, 1)
            sp.wait_ge(lists_ready, 16 * TT * TOPK)
            sp.dma_start(g_fin_row[:, :], final_norm_g.partition_broadcast(P)).then_inc(g_fin_loaded, 16)
            stored, used = fixed(sp, end * 16), fixed(sp, end * JOB)
            sp.wait_ge(y_stored, stored)
            sp.wait_ge(w_hi_ready, used)
            sp.wait_ge(w_lo_ready, used)
            for t in range(TT):
                sp.dma_start(raw01[:, t, 0:D_MODEL], sum_rows[t * P:(t + 1) * P, :]).then_inc(sum_loaded[t], 16)
            for t in range(TT):
                sp.wait_ge(out_ready, t + 1)
                sp.dma_start(out[0, t * P:(t + 1) * P, :], raw01[:, t, 0:D_MODEL]).then_inc(out_stored, 16)
            sp.wait_ge(out_stored, 16 * TT)

        @block.gpsimd
        def _(pool):
            steps = 0

            def made(ins):
                nonlocal steps
                steps += 1
                ins.then_inc(pool_step, 1)
                pool.wait_ge(pool_step, steps)

            pool.iota(diff[:, :], pattern=[[-1, W]], base=(TT - 1) * P, channel_multiplier=1).then_inc(consts_made, 1)
            pool.memset(ident[:, :], 0.0).then_inc(pool_step, 1)
            steps += 1
            pool.wait_ge(pool_step, steps)
            pool.affine_select(out=ident[:, :], in_=ident[:, :], compare_op=ALU.not_equal, fill=1.0, base=0,
                               pattern=[[-1, P]], channel_multiplier=1).then_inc(consts_made, 1)
            pool.memset(ones[:, :], 1.0).then_inc(consts_made, 1)
            pool.memset(z_sb[:, :], 0.0).then_inc(consts_made, 1)
            half = [w // 2 for w, _ in BRANCHES]
            pool.wait_ge(bits_ready, 3)
            made(pool.tensor_scalar(seen[:, :], absd[:, :], float(half[0]), None, ALU.is_le))
            for step, reach in ((step4, half[1]), (step16, half[2])):
                made(pool.tensor_scalar(seen_b[:, :], step[:, :], 0, None, ALU.is_equal))
                if reach < SEQ:
                    made(pool.tensor_scalar(seen_c[:, :], absd[:, :], float(reach), None, ALU.is_le))
                    made(pool.tensor_tensor(seen_b[:, :], seen_b[:, :], seen_c[:, :], ALU.mult))
                made(pool.tensor_tensor(seen[:, :], seen[:, :], seen_b[:, :], ALU.add))
            inv = HEAD_DIM ** 0.5
            made(pool.tensor_scalar(log_m[:, :], seen[:, :], 0.0, MASKED, ALU.is_equal, ALU.mult))
            for m in range(2, len(BRANCHES) + 1):
                made(pool.tensor_scalar(seen_b[:, :], seen[:, :], float(m), math.log(m) * inv,
                                        ALU.is_equal, ALU.mult))
                made(pool.tensor_tensor(log_m[:, :], log_m[:, :], seen_b[:, :], ALU.add))
            def bias(h):
                slope = 2.0 ** (-8.0 * (h + 1) / HEADS)
                if h >= 2:
                    pool.wait_ge(scores_taken, (h - 1) * TT)
                made(pool.tensor_scalar(bias_h[:, h % 2, :], absd[:, :], -slope * HEAD_DIM ** 0.5, None, ALU.mult))
                pool.tensor_tensor(bias_h[:, h % 2, :], bias_h[:, h % 2, :], log_m[:, :], ALU.add)\
                    .then_inc(bias_ready, 1)

            bias(0)

            per_p = [(g_merge[:, 0:NA], attn_out_norm_g[0].rearrange("(k p) -> p k", p=P)),
                     (g_merge[:, NA:KD], conv_out_norm_g[0].rearrange("(k p) -> p k", p=P)),
                     (g_ffn[:, :], ffn_norm_g[0].rearrange("(k p) -> p k", p=P)),
                     (conv_c[:, 0, :], conv_w[0, 0].rearrange("(k p) -> p k", p=P)),
                     (conv_c[:, 1, :], conv_w[0, 1].rearrange("(k p) -> p k", p=P)),
                     (conv_c[:, 2, :], conv_w[0, 2].rearrange("(k p) -> p k", p=P)),
                     (g_ffn_row[:, :], ffn_norm_g[0].partition_broadcast(P)),
                     (b_r[:, :], b_router[0].partition_broadcast(P)),
                     (w_r[:, :, :], w_router[0].rearrange("(k p) e -> p k e", p=P))]
            for dst, src in per_p:
                pool.dma_start(dst, src, allow_slow_non_contiguous=True).then_inc(params_loaded, 16)

            made(pool.memset(sel_all[:, :], 0.0))
            for half in range(2):
                pool.affine_select(out=sel_all[:, :], in_=sel_all[:, :], compare_op=ALU.not_equal, fill=1.0,
                                   base=-half * E, pattern=[[-1, E]], channel_multiplier=1).then_inc(sel_all_made, 1)
                pool.wait_ge(sel_all_made, half + 1)

            def convolve(c):
                dst = merged[:, NA + c, :]
                pool.wait_ge(proj_taken, conv_tile(CONV_DONE[c]) + 1)
                made(pool.tensor_tensor(z_sb[:, 1:SEQ + 1], gc_sb[:, :], u_sb[:, c % 2, :], ALU.mult))
                made(pool.tensor_scalar(dst, z_sb[:, 0:SEQ], conv_c[:, 0, c:c + 1], None, ALU.mult))
                for i in (1, 2):
                    made(pool.tensor_scalar(tap[:, :], z_sb[:, i:SEQ + i], conv_c[:, i, c:c + 1], None, ALU.mult))
                    made(pool.tensor_tensor(dst, dst, tap[:, :], ALU.add))
                pool.tensor_tensor(dst, dst, gb_sb[:, :], ALU.mult).then_inc(conv_ready, 1)
                pool.wait_ge(conv_ready, c + 1)

            pool.wait_ge(params_loaded, 16 * 9)
            for h in range(1, HEADS):
                bias(h)
                if h == 5:
                    convolve(0)
            for c in range(1, NC_):
                convolve(c)
            pool.wait_ge(scores_ready, HEADS * TT)
            for t in range(TT):
                pool.dma_start(x1[:, t, :], x[0, t * P:(t + 1) * P, :]).then_inc(x_again, 16)

            pool.wait_ge(heads_ready, HEADS)
            made(pool.memset(empty[:, :], NONE))
            pool.dma_start(lists.rearrange("(p r) c -> p (r c)", p=P), empty[:, :]).then_inc(lists_emptied, 16)
            pool.iota(iota_e[:, :], pattern=[[1, E]], base=0, channel_multiplier=0,
                      allow_small_or_imprecise_dtypes=True).then_inc(consts_made, 1)
            pool.iota(base_e[:, :], pattern=[[LIST, E]], base=0, channel_multiplier=0,
                      allow_small_or_imprecise_dtypes=True).then_inc(consts_made, 1)
            pool.iota(token[:, :], pattern=[[P, TT]], base=-NONE, channel_multiplier=1,
                      allow_small_or_imprecise_dtypes=True).then_inc(consts_made, 1)
            made(pool.memset(before[:, :], 1.0))
            pool.affine_select(out=before[:, :], in_=before[:, :], compare_op=ALU.is_gt, fill=0.0, base=0,
                               pattern=[[1, P]], channel_multiplier=-1).then_inc(consts_made, 1)
            made(pool.memset(entry[:, :, :], 0))
            pool.iota(entry[:, :, 0].bitcast(I32), pattern=[[P, TT], [0, TOPK]], base=0, channel_multiplier=1)\
                .then_inc(entry_made, 1)
            wait_used(pool, N_FRONT - 1)
            pool.iota(iota_n[:, :], pattern=[[1, TILE]], base=0, channel_multiplier=0,
                      allow_small_or_imprecise_dtypes=True).then_inc(iota_n_made, 1)
            pool.memset(x_got[:, :], 0.0).then_inc(x_got_cleared, 1)
            for t in range(2, TT):
                pool.wait_ge(xn_scaled, t + 1)
                pool.tensor_tensor(xn[:, t, :], xn[:, t, :], g_ffn_row[:, :], ALU.mult).then_inc(xn_pool_ready, 1)

            last_token = pool.to_reg(SEQ - 1)

            def list_row(j):
                return fixed(pool, expert(j) * LIST + round_(j) * TILE)

            def load_list(dst, row, done):
                pool.dma_start(dst[0:TILE, :], lists[bass.ds(row, TILE), :]).then_inc(done, 16)

            def gather(j):
                row, lists_, turns = list_row(j), fixed(pool, j * 16 - 16), fixed(pool, j * 2)
                pool.wait_ge(x_gathered, j * 16 - 16)
                load_list(gather_list, row, gather_list_loaded)
                pool.wait_ge(xn_stored, 16 * TT)
                pool.wait_ge(gather_list_loaded, lists_)
                pool.wait_ge(got_turned, turns)
                gather_rows()

            def gather_rows():
                pool.indirect_dma_start(out=x_got[0:TILE, :], out_offset=None, in_=xn_rows,
                                        in_offset=bass.IndirectOffsetOnAxis(ap=gather_list[0:TILE, 0:1], axis=0),
                                        bounds_check=last_token, oob_is_err=False).then_inc(x_gathered, 16)

            def scatter(j):
                done = fixed(pool, j + 1)
                pool.wait_ge(x1_stored, 16 * TT)
                pool.wait_ge(lists_ready, 16 * TT * TOPK)
                pool.wait_ge(y_half_ready, done)
                pool.wait_ge(y_ready, done)
                pool.indirect_dma_start(out=sum_rows, in_=y_out[0:TILE, :], in_offset=None,
                                        out_offset=bass.IndirectOffsetOnAxis(ap=scatter_list[0:TILE, 0:1], axis=0),
                                        bounds_check=last_token, oob_is_err=False,
                                        compute_op=ALU.add).then_inc(y_stored, 16)

            def load_scatter_list(j):
                row = list_row(j)
                if not (isinstance(j, int) and j == 0):
                    pool.wait_ge(y_stored, j * 16)
                load_list(scatter_list, row, scatter_list_loaded)

            pool.wait_ge(x_got_cleared, 1)
            pool.wait_ge(xn_stored, 16 * TT)
            pool.wait_ge(list_1_ready, 1)
            gather_rows()

            last_place = pool.to_reg(ROWS - 1)
            pool.wait_ge(lists_emptied, 16)
            pool.wait_ge(entry_made, 1)
            pool.wait_ge(entry_ready, 1)
            for n in range(TT * TOPK):
                pool.indirect_dma_start(out=lists, out_offset=bass.IndirectOffsetOnAxis(ap=dest[:, n:n + 1], axis=0),
                                        in_=entry[:, n, :], in_offset=None, bounds_check=last_place,
                                        oob_is_err=False).then_inc(lists_ready, 16)
            pool.wait_ge(lists_ready, 16 * TT * TOPK)

            def job(j, first=False):
                gather(j + 1)
                if not first:
                    scatter(j - 2)
                load_scatter_list(j - 1)

            job(1, first=True)
            end = jobs_end(pool)
            with pool.Fori(2, end) as j:
                job(j)
            scatter(end - 2)
            load_scatter_list(end - 1)
            scatter(end - 1)
            pool.wait_ge(y_stored, end * 16)
            pool.wait_ge(x_gathered, end * 16)

        @block.scalar
        def _(act):
            act.dma_start(g_mix[:, :], mix_norm_g[0].rearrange("(k p) -> p k", p=P),
                          allow_slow_non_contiguous=True).then_inc(g_mix_loaded, 16)

            for t in range(TT):
                act.wait_ge(x_loaded[t], 16)
                if t:
                    act.wait_ge(ss_x_ready, t)
                act.activation(sq_x[:, :], x_sb[:, t, :], ACT.Square, accum_out=ss_x[:, t:t + 1])\
                   .then_inc(ss_x_ready, 1)
                act.wait_ge(var_x_ready, t + 1)
                act.activation(std_x[:, t:t + 1], std_x[:, t:t + 1], ACT.Sqrt).then_inc(std_x_ready, 1)

            def split_front(s):
                act.wait_ge(front_loaded[s % RAW_FRONT], 32 * (s // RAW_FRONT + 1))
                if s >= SPLIT_FRONT:
                    wait_used(act, s - SPLIT_FRONT)
                act.activation(hi01[:, s % SPLIT_FRONT, :], raw01[:, s % RAW_FRONT, :], ACT.Copy)\
                   .then_inc(front_hi, 1)

            split_front(0)
            act.wait_ge(g_mix_loaded, 16)
            for k in range(KD):
                act.wait_ge(xT_turned, k + 1)
                act.activation(xnT_hi[:, k, :], bank[k][:, :], ACT.Copy, scale=g_mix[:, k:k + 1])\
                   .then_inc(xnT_hi_ready, 1)
            split_front(1)

            def take(s, n):
                i, kind = first_tile[s] + n, chunks[s][0]
                if kind == "conv":
                    return
                act.wait_ge(proj_ready, i + 1)
                if kind == "v":
                    dst, src = v_hi[:, n, (s - 1) * 2 * P:s * 2 * P], bank[i % 2][:, 0:2 * P]
                else:
                    dst, src = qk_hi[:, chunks[s][1] % 2, n, :], bank[i % 2][:, :]
                act.activation(dst, src, ACT.Copy).then_inc(proj_hi_ready, 1)

            for s in range(3):
                for n in range(tiles_of[s]):
                    take(s, n)
                if s < 2:
                    split_front(s + 2)

            def take_head(h):
                half = slice(HEAD_DIM * (h % 2), HEAD_DIM * (h % 2) + HEAD_DIM)
                act.wait_ge(heads_ready, h + 1)
                act.activation(merged[half, h // 2, :], bank[6][half, :], ACT.Copy).then_inc(heads_taken, 1)
                if h % 2:
                    act.wait_ge(heads_taken, h + 1)
                    if h > 1:
                        act.wait_ge(sq_attn_summed, h // 2)
                    act.activation(sq_sb[:, 0, :], merged[:, h // 2, :], ACT.Square).then_inc(sq_attn_ready, 1)

            def square_conv(c):
                act.wait_ge(conv_ready, c + 1)
                if c:
                    act.wait_ge(sq_conv_summed, c)
                act.activation(sq_sb[:, 1, :], merged[:, NA + c, :], ACT.Square).then_inc(sq_conv_ready, 1)

            for h in range(HEADS):
                s = 3 + h
                if h:
                    take(s - 1, 1)
                split_front(s + 1)
                act.wait_ge(max_ready, h + 1)
                for t in range(TT):
                    act.activation(probs[:, t, :], probs[:, t, :], ACT.Exp, bias=neg_max[:, h * TT + t:h * TT + t + 1],
                                   scale=HEAD_DIM ** -0.5, accum_out=den[:, h * TT + t:h * TT + t + 1])\
                       .then_inc(exp_ready, 1)
                take(s, 0)
                if h:
                    take_head(h - 1)
                for c in range(TT):
                    act.wait_ge(probs_turned, h * TT + c + 1)
                    act.activation(pT_hi[:, c, :], bank[4 + c % 2][:, :], ACT.Copy).then_inc(pT_hi_ready, 1)
                if h in (5, 7):
                    square_conv((h - 5) // 2)
            take(N_IN - 2, 1)
            take_head(HEADS - 1)
            split_front(N_IN)
            square_conv(2)

            def split(m, slot_no, loads):
                act.wait_ge(w_loaded[slot_no % RAW], loads * 16)
                if isinstance(m, int) and m < SPLIT:
                    wait_split_slot(act, m)
                else:
                    act.wait_ge(w_used, m - (SPLIT - 1))
                act.activation(hi_slot(slot_no % SPLIT), raw_slot(slot_no % RAW), ACT.Copy).then_inc(w_hi_ready, 1)

            wait_used(act, N_IN - 1)
            act.wait_ge(params_loaded, 16 * 9)

            def split_merged(k):
                if k >= NA:
                    act.wait_ge(conv_ready, k - NA + 1)
                act.activation(mT_hi[:, k, :], merged[:, k, :], ACT.Copy, scale=g_merge[:, k:k + 1])\
                   .then_inc(mT_hi_ready, 1)

            act.wait_ge(heads_taken, HEADS)
            for k in range(NA):
                split_merged(k)
            split_front(N_IN + 1)
            square_conv(3)
            for k in range(NA, KD):
                split_merged(k)
            act.wait_ge(var_g_ready, 1)
            act.activation(std_g, std_g, ACT.Sqrt).then_inc(std_g_ready, 1)
            act.wait_ge(probs_turned, HEADS * TT)
            for half in range(2):
                rows = slice(half * E, half * E + E)
                act.dma_start(b_raw_gu[rows, :], b_gate_up[0]).then_inc(b_loaded, 16)
                act.dma_start(b_raw_dn[rows, :], b_down[0]).then_inc(b_loaded, 16)
            split_front(N_IN + 2)
            act.wait_ge(b_loaded, 64)
            act.activation(b_hl[:, 0:2 * D_FF], b_raw_gu[:, :], ACT.Copy).then_inc(b_hi_ready, 1)
            act.activation(b_hl[:, 2 * D_FF:3 * D_FF], b_raw_dn[:, :], ACT.Copy).then_inc(b_hi_ready, 1)
            split_front(N_IN + 3)
            split(0, 0, 1)
            split(1, 1, 1)

            def square_x1(t):
                act.wait_ge(mix_taken, TT * 2 + 2 * t + 2)
                act.dma_start(sum_rows[t * P:(t + 1) * P, :], x1[:, t, :]).then_inc(x1_stored, 16)
                if t:
                    act.wait_ge(ss_1_ready, t)
                act.activation(sq_x1[:, :], x1[:, t, :], ACT.Square, accum_out=ss_1[:, t:t + 1])\
                   .then_inc(ss_1_ready, 1)

            def take_x1T(t):
                act.wait_ge(x1_turned, 2 * t + 1)
                act.activation(x1T[:, 0:TT, t * P:(t + 1) * P],
                               bank[2 * t][:, :].rearrange("p (k n) -> p k n", k=TT), ACT.Copy)\
                   .then_inc(x1T_act_ready, 1)

            square_x1(0)
            square_x1(1)
            take_x1T(0)
            square_x1(2)
            take_x1T(1)
            square_x1(3)
            take_x1T(2)
            take_x1T(3)
            act.wait_ge(var_1_ready, 1)
            act.activation(std_1, std_1, ACT.Sqrt).then_inc(std_1_ready, 1)
            act.wait_ge(rstd_1_ready, 1)
            act.wait_ge(x1_turned, 2 * TT)
            act.wait_ge(x1_stored, 16 * TT)
            for t in range(TT):
                act.activation(xn[:, t, :], x1[:, t, :], ACT.Copy, scale=rstd_1[:, t:t + 1]).then_inc(xn_scaled, 1)
            split(2, 2, 1)
            act.wait_ge(gate_shift_ready, 1)
            act.activation(gexp[:, :, :], gexp[:, :, :], ACT.Exp).then_inc(gate_exp_ready, 1)
            for t in range(TT):
                if t < 2:
                    act.wait_ge(xn_dve_ready, t + 1)
                else:
                    act.wait_ge(xn_pool_ready, t - 1)
                act.dma_start(xn_rows[t * P:(t + 1) * P, :], xn[:, t, :]).then_inc(xn_stored, 16)

            def gu(j, i):
                split(gu_chunk(j, i), GU[i], loads_of(j - 1, GU[i]))

            def dn(j, i):
                split(dn_chunk(j, i), DN[i], loads_of(j, DN[i]))

            def loads_of(jobs, slot_no):
                return jobs * (JOB // RAW) + (slot_no // RAW + 1)

            def turned(j, hi, bank_ready, hi_ready):
                for g in range(2):
                    act.wait_ge(bank_ready, j * 2 + (g + 1))
                    act.activation(hi[:, g * TT:(g + 1) * TT, :].rearrange("p k n -> p (k n)"), bank[6 + g][:, 0:TT * TILE],
                                   ACT.Copy).then_inc(hi_ready, 1)

            def sigmoid(j):
                act.wait_ge(gu_clamped, j * 2 + 1)
                if not (isinstance(j, int) and j == 0):
                    act.wait_ge(act_ready, j)
                act.activation(sig_in[0:TILE, :], gate_in[0:TILE, :], ACT.Sigmoid, scale=ALPHA).then_inc(sig_ready, 1)

            def take_y(j):
                act.wait_ge(scatter_list_loaded, j * 16 + 16)
                for g in range(2):
                    if g == 0:
                        act.wait_ge(w_used, y_chunks(j))
                    act.activation(y_out[0:TILE, g * 512:(g + 1) * 512], bank[4 + g][0:TILE, :], ACT.Copy,
                                   scale=scatter_list[0:TILE, 1:2].bitcast(F32)).then_inc(y_half_ready if g == 0 else y_ready, 1)

            def y_chunks(j):
                return j * JOB + (2 * GU_CHUNKS + DN_CHUNKS)

            turned(0, xT_hi, got_turned, xT_hi_ready)
            for i in range(SPLIT, GU_CHUNKS):
                split(i, i, i // RAW + 1)

            def job(j, first=False, final=False):
                gu(j, 0)
                if first:
                    turned(1, xT_hi, got_turned, xT_hi_ready)
                sigmoid(j - 1)
                gu(j, 1)
                gu(j, 2)
                if not first:
                    take_y(j - 2)
                for i in range(3, 7):
                    gu(j, i)
                turned(j - 1, aT_hi, act_turned, aT_hi_ready)
                gu(j, 7)
                for i in range(3):
                    dn(j - 1, i)
                if final:
                    sigmoid(j)
                else:
                    turned(j + 1, xT_hi, got_turned, xT_hi_ready)
                dn(j - 1, 3)

            job(1, first=True)
            end = jobs_end(act)
            with act.Fori(2, end - 1) as j:
                job(j)
            last = act.snap(end - 1)
            job(last, final=True)
            turned(last, xT_hi, act_turned, aT_hi_ready)
            split(last_dn_chunk(last, 0), DN_LAST[0], loads_of(last, DN_LAST[0]))
            take_y(end - 2)
            for i in range(1, DN_CHUNKS):
                split(last_dn_chunk(last, i), DN_LAST[i], loads_of(last, DN_LAST[i]))
            act.wait_ge(scatter_list_loaded, end * 16)
            act.wait_ge(y_stored, end * 16 - 16)
            act.wait_ge(w_used, end * JOB)
            act.activation(y_out[0:TILE, 0:512], bank[4][0:TILE, :], ACT.Copy,
                           scale=scatter_list[0:TILE, 1:2].bitcast(F32)).then_inc(y_half_ready, 1)
            act.activation(y_out[0:TILE, 512:1024], bank[5][0:TILE, :], ACT.Copy,
                           scale=scatter_list[0:TILE, 1:2].bitcast(F32)).then_inc(y_ready, 1)

            act.activation(std_f[:, 0:1], ss_1[:, 0:1], ACT.Sqrt)
            for t in range(TT):
                act.wait_ge(sum_loaded[t], 16)
                if t:
                    act.wait_ge(ss_f_ready, t)
                act.activation(y_out[:, :], raw01[:, t, 0:D_MODEL], ACT.Square, accum_out=ss_f[:, t:t + 1])\
                   .then_inc(ss_f_ready, 1)
                act.wait_ge(var_f_ready, t + 1)
                act.activation(std_f[:, t:t + 1], std_f[:, t:t + 1], ACT.Sqrt).then_inc(std_f_ready, 1)

        @block.vector
        def _(dve):
            steps = 0

            def did(ins):
                nonlocal steps
                steps += 1
                ins.then_inc(dve_step, 1)
                dve.wait_ge(dve_step, steps)

            dve.wait_ge(consts_made, 1)
            dve.tensor_scalar(step4[:, :], diff[:, :], BRANCHES[1][1] - 1, None, ALU.bitwise_and)\
               .then_inc(bits_ready, 1)
            dve.tensor_scalar(step16[:, :], diff[:, :], BRANCHES[2][1] - 1, None, ALU.bitwise_and)\
               .then_inc(bits_ready, 1)
            did(dve.tensor_copy(absd[:, :], diff[:, :]))
            dve.scalar_tensor_tensor(absd[:, :], absd[:, :], -1.0, absd[:, :], ALU.mult, ALU.max)\
               .then_inc(bits_ready, 1)

            dve.wait_ge(consts_made, 2)
            for t in range(TT):
                dve.wait_ge(ss_x_ready, t + 1)
                dve.tensor_scalar(std_x[:, t:t + 1], ss_x[:, t:t + 1], 1.0 / D_MODEL, EPS, ALU.mult, ALU.add)\
                   .then_inc(var_x_ready, 1)
                dve.wait_ge(std_x_ready, t + 1)
                dve.reciprocal(rstd_x[:, t:t + 1], std_x[:, t:t + 1]).then_inc(rstd_x_ready, 1)
                dve.wait_ge(rstd_x_ready, t + 1)
                dve.tensor_scalar(diag[:, t, :], ident[:, :], rstd_x[:, t:t + 1], None, ALU.mult)\
                   .then_inc(diag_ready, 1)

            def split_front(s):
                dve.wait_ge(front_hi, s + 1)
                dve.wait_ge(front_loaded[s % RAW_FRONT], 32 * (s // RAW_FRONT + 1))
                if s >= SPLIT_FRONT:
                    wait_used(dve, s - SPLIT_FRONT)
                dve.tensor_tensor(lo01[:, s % SPLIT_FRONT, :], raw01[:, s % RAW_FRONT, :],
                                  hi01[:, s % SPLIT_FRONT, :], ALU.subtract).then_inc(front_lo, 1)

            split_front(0)
            dve.wait_ge(g_mix_loaded, 16)
            for k in range(KD):
                dve.wait_ge(xnT_hi_ready, k + 1)
                dve.scalar_tensor_tensor(xnT_lo[:, k, :], bank[k][:, :], g_mix[:, k:k + 1], xnT_hi[:, k, :],
                                         ALU.mult, ALU.subtract).then_inc(xnT_lo_ready, 1)
            split_front(1)

            def take(s, n):
                i, kind = first_tile[s] + n, chunks[s][0]
                if kind == "conv":
                    c = sum(x[0] == "conv" for x in chunks[:s]) * 2 + n
                    name, ch = CONV_TILES[c]
                    dst = {"gb": gb_sb[:, :], "gc": gc_sb[:, :], "u": u_sb[:, ch % 2, :]}[name]
                    if ch and name != "u" or name == "u" and ch > 1:
                        dve.wait_ge(conv_ready, ch if name != "u" else ch - 1)
                    dve.wait_ge(proj_ready, i + 1)
                    dve.tensor_copy(dst, bank[i % 2][:, :]).then_inc(proj_taken, 1)
                    return
                dve.wait_ge(proj_hi_ready, splits_to(i))
                if kind == "v":
                    cols = slice((s - 1) * 2 * P, s * 2 * P)
                    out_, src, hi = v_lo[:, n, cols], bank[i % 2][:, 0:2 * P], v_hi[:, n, cols]
                else:
                    b = chunks[s][1] % 2
                    out_, src, hi = qk_lo[:, b, n, :], bank[i % 2][:, :], qk_hi[:, b, n, :]
                dve.tensor_tensor(out_, src, hi, ALU.subtract).then_inc(proj_taken, 1)

            for s in range(3):
                for n in range(tiles_of[s]):
                    take(s, n)
                if s < 2:
                    split_front(s + 2)

            for h in range(HEADS):
                s = 3 + h
                dve.wait_ge(bias_ready, h + 1)
                if h:
                    dve.wait_ge(probs_turned, h * TT)
                for t in range(TT):
                    dve.wait_ge(scores_ready, h * TT + t + 1)
                    shift = (TT - 1 - t) * P
                    dve.tensor_tensor_reduce(probs[:, t, :], bank[2 + t % 2][:, :], bias_h[:, h % 2, shift:shift + SEQ],
                                             1.0, -3.0e38, ALU.add, ALU.max, max_s[:, h * TT + t:h * TT + t + 1])\
                       .then_inc(scores_taken, 1)
                dve.wait_ge(scores_taken, (h + 1) * TT)
                cols = slice(h * TT, (h + 1) * TT)
                dve.tensor_scalar(neg_max[:, cols], max_s[:, cols], -HEAD_DIM ** -0.5, None, ALU.mult)\
                   .then_inc(max_ready, 1)
                if h:
                    take(s - 1, 1)
                split_front(s + 1)
                dve.wait_ge(exp_ready, (h + 1) * TT)
                did(dve.reciprocal(rden[:, cols], den[:, cols]))
                for t in range(TT):
                    dve.tensor_scalar(probs[:, t, :], probs[:, t, :], rden[:, h * TT + t:h * TT + t + 1], None,
                                      ALU.mult).then_inc(probs_ready, 1)
                take(s, 0)
                for c in range(TT):
                    dve.wait_ge(pT_hi_ready, h * TT + c + 1)
                    dve.tensor_tensor(pT_lo[:, c, :], bank[4 + c % 2][:, :], pT_hi[:, c, :], ALU.subtract)\
                       .then_inc(pT_lo_ready, 1)
            take(N_IN - 2, 1)
            take(N_IN - 1, 0)
            split_front(N_IN)
            take(N_IN - 1, 1)

            def split(m, slot_no):
                dve.wait_ge(w_hi_ready, m + 1)
                if isinstance(m, int) and m < SPLIT:
                    wait_split_slot(dve, m)
                else:
                    dve.wait_ge(w_used, m - (SPLIT - 1))
                dve.tensor_tensor(lo_slot(slot_no % SPLIT), raw_slot(slot_no % RAW), hi_slot(slot_no % SPLIT),
                                  ALU.subtract).then_inc(w_lo_ready, 1)

            def select(dst, j, ready, used):
                column = sel_all[:, bass.ds(fixed(dve, expert(j)), 1)].to_broadcast([2 * E, TILE])
                if not (isinstance(j, int) and j == 0):
                    dve.wait_ge(used, j)
                dve.tensor_scalar(dst[:, :], column, 1.0, None, ALU.mult).then_inc(ready, 1)

            def turned(j, hi, lo, hi_ready, lo_ready):
                for g in range(2):
                    dve.wait_ge(hi_ready, j * 2 + (g + 1))
                    rows = slice(g * TT, (g + 1) * TT)
                    dve.tensor_tensor(lo[:, rows, :].rearrange("p k n -> p (k n)"), bank[6 + g][:, 0:TT * TILE],
                                      hi[:, rows, :].rearrange("p k n -> p (k n)"), ALU.subtract).then_inc(lo_ready, 1)

            def split_merged(k):
                dve.wait_ge(mT_hi_ready, k + 1)
                dve.scalar_tensor_tensor(mT_lo[:, k, :], merged[:, k, :], g_merge[:, k:k + 1], mT_hi[:, k, :],
                                         ALU.mult, ALU.subtract).then_inc(mT_lo_ready, 1)

            for k in range(NA):
                split_merged(k)
            split_front(N_IN + 1)
            for k in range(NA, KD):
                split_merged(k)
            dve.wait_ge(sq_attn_summed, NA)
            dve.wait_ge(sq_conv_summed, NC_)
            dve.tensor_reduce(ss_g, bank[7][:, 0:TT * KD].rearrange("p (t g k) -> p t g k", t=TT, g=2),
                                  AX.X, ALU.add).then_inc(sums_taken, 1)
            dve.wait_ge(sums_taken, 1)
            dve.tensor_scalar(std_g, ss_g, 1.0 / AW, EPS, ALU.mult, ALU.add).then_inc(var_g_ready, 1)
            dve.wait_ge(std_g_ready, 1)
            did(dve.reciprocal(rstd_g, std_g))
            split_front(N_IN + 2)
            dve.wait_ge(x_again, 16 * TT)
            for t in range(TT):
                for n in range(2):
                    dve.wait_ge(mix_ready, 2 * t + n + 1)
                    dst = x1[:, t, n * 512:(n + 1) * 512]
                    dve.scalar_tensor_tensor(dst, bank[2 * t + n][:, :], rstd_g[:, 2 * t:2 * t + 1], dst,
                                             ALU.mult, ALU.add).then_inc(mix_taken, 1)
            split_front(N_IN + 3)

            split(0, 0)
            for k in range(KD):
                ins = dve.tensor_scalar(w_r[:, k, :], w_r[:, k, :], g_ffn[:, k:k + 1], None, ALU.mult)
            ins.then_inc(w_r_ready, 1)
            dve.wait_ge(b_hi_ready, 2)
            for raw, cols in ((b_raw_gu, slice(0, 2 * D_FF)), (b_raw_dn, slice(2 * D_FF, 3 * D_FF))):
                ins = dve.tensor_tensor(b_hl[E:2 * E, cols], raw[E:2 * E, :], b_hl[E:2 * E, cols], ALU.subtract)
            ins.then_inc(b_ready, 1)

            def add_conv(t):
                for n in range(2):
                    dve.wait_ge(mix_ready, 2 * TT + 2 * t + n + 1)
                    dve.wait_ge(mix_taken, 2 * TT)
                    dst = x1[:, t, n * 512:(n + 1) * 512]
                    dve.scalar_tensor_tensor(dst, bank[2 * t + n][:, :], rstd_g[:, 2 * t + 1:2 * t + 2], dst,
                                             ALU.mult, ALU.add).then_inc(mix_taken, 1)

            def take_x1T(t):
                dve.wait_ge(x1_turned, 2 * t + 2)
                dve.tensor_copy(x1T[:, TT:KD, t * P:(t + 1) * P],
                                bank[2 * t + 1][:, :].rearrange("p (k n) -> p k n", k=TT)).then_inc(x1T_dve_ready, 1)

            add_conv(0)
            split(1, 1)
            add_conv(1)
            take_x1T(0)
            add_conv(2)
            take_x1T(1)
            add_conv(3)
            take_x1T(2)
            take_x1T(3)
            dve.wait_ge(ss_1_ready, TT)
            dve.tensor_scalar(std_1, ss_1, 1.0 / D_MODEL, EPS, ALU.mult, ALU.add).then_inc(var_1_ready, 1)
            dve.wait_ge(std_1_ready, 1)
            dve.reciprocal(rstd_1, std_1).then_inc(rstd_1_ready, 1)
            dve.wait_ge(rstd_1_ready, 1)
            dve.wait_ge(consts_made, 8)
            for t in range(TT):
                dve.wait_ge(router_ready, t + 1)
                did(dve.scalar_tensor_tensor(logits[:, t, :], bank[2 * t][:, 0:E], rstd_1[:, t:t + 1], b_r[:, :],
                                             ALU.mult, ALU.add))
                did(dve.max(top_v[:, t, :], logits[:, t, :]))
                did(dve.max_index(top_i[:, t, :], top_v[:, t, :], logits[:, t, :]))
                did(dve.tensor_copy(top_f[:, t, :], top_i[:, t, 0:TOPK]))
                did(dve.tensor_tensor(chosen[:, t, :, :], iota_e[:, :].unsqueeze(1).to_broadcast([P, TOPK, E]),
                                      top_f[:, t, :].unsqueeze(2).to_broadcast([P, TOPK, E]), ALU.is_equal))
                dve.tensor_reduce(mask[:, t, :], chosen[:, t, :, :].rearrange("p k e -> p e k"), AX.X, ALU.add)\
                   .then_inc(mask_ready, 1)
            dve.tensor_tensor(gexp[:, :, :], top_v[:, :, 0:TOPK], top_v[:, :, 0:1].to_broadcast([P, TT, TOPK]),
                              ALU.subtract).then_inc(gate_shift_ready, 1)

            def gain_xn(t):
                dve.wait_ge(xn_scaled, t + 1)
                dve.tensor_tensor(xn[:, t, :], xn[:, t, :], g_ffn_row[:, :], ALU.mult).then_inc(xn_dve_ready, 1)

            gain_xn(0)
            dve.wait_ge(router_ready, TT)
            dve.wait_ge(rank_ready, 1)
            dve.wait_ge(mask_ready, TT)
            did(dve.tensor_tensor(rank[:, :, :], bank[1][:, 0:TT * E].rearrange("p (t e) -> p t e", t=TT),
                                  base_e[:, :].unsqueeze(1).to_broadcast([P, TT, E]), ALU.add))
            dve.wait_ge(iota_n_made, 1)
            for t in range(TT):
                dve.tensor_scalar(pick[:, t, :], iota_n[:, :], rank[:, t, 0:1], mask[:, t, 0:1],
                                  ALU.is_equal, ALU.mult).then_inc(pick_ready, 1)
            gain_xn(1)
            dve.tensor_tensor(token_1[:, :], token[:, :], mask[:, :, 1], ALU.mult).then_inc(pick_1_ready, 1)
            for t in range(TT):
                dve.tensor_scalar(pick_1[:, t, :], iota_n[:, :], float(LIST), rank[:, t, 1:2],
                                  ALU.add, ALU.is_equal).then_inc(pick_1_ready, 1)
            for t in range(TT):
                did(dve.tensor_tensor(chosen_p[:, t, :, :], chosen[:, t, :, :],
                                      rank[:, t, :].unsqueeze(1).to_broadcast([P, TOPK, E]), ALU.mult))
            dve.wait_ge(places_1_ready, 1)
            dve.tensor_scalar(gather_list[0:TILE, 0:1], bank[4][0:TILE, 0:1], float(NONE), None, ALU.add)\
               .then_inc(list_1_ready, 1)
            did(dve.tensor_reduce(dest_f[:, :], chosen_p[:, :, :, :].rearrange("p t k e -> p (t k) e"), AX.X, ALU.add))
            did(dve.tensor_copy(dest[:, :], dest_f[:, :]))
            dve.wait_ge(gate_exp_ready, 1)
            did(dve.tensor_reduce(gsum[:, 0, :], gexp[:, :, :], AX.X, ALU.add))
            did(dve.reciprocal(gsum[:, 1, :], gsum[:, 0, :]))
            dve.wait_ge(entry_made, 1)
            for t in range(TT):
                ins = dve.tensor_scalar(entry[:, t * TOPK:(t + 1) * TOPK, 1].bitcast(F32), gexp[:, t, :],
                                        gsum[:, 1, t:t + 1], None, ALU.mult)
            ins.then_inc(entry_ready, 1)
            dve.wait_ge(sel_all_made, 2)
            select(sel_gu, 0, sel_gu_ready, sel_gu_used)
            turned(0, xT_hi, xT_lo, xT_hi_ready, xT_lo_ready)
            split(2, 2)
            dve.wait_ge(counts_ready, 1)
            did(dve.tensor_reduce(cnt_f[:, 0:1], bank[5][:, 0:E], AX.X, ALU.max))
            did(dve.tensor_scalar(cnt_f[:, 1:2], cnt_f[:, 0:1], float(TILE), None, ALU.is_gt))
            for r in range(2, ROUNDS):
                did(dve.scalar_tensor_tensor(cnt_f[:, 1:2], cnt_f[:, 0:1], float(r * TILE), cnt_f[:, 1:2],
                                             ALU.is_gt, ALU.add))
            dve.tensor_copy(extra_sb[:, :], cnt_f[:, 1:2]).then_inc(extra_ready, 1)

            def gu(j, i):
                split(gu_chunk(j, i), GU[i])

            def dn(j, i):
                split(dn_chunk(j, i), DN[i])

            def clamp(j, used):
                dve.wait_ge(w_used, used)
                if not (isinstance(j, int) and j == 0):
                    dve.wait_ge(act_turned, j * 2)
                for n in range(2):
                    ins = dve.tensor_scalar(gate_in[0:TILE, n * 512:(n + 1) * 512], bank[n][0:TILE, :], LIMIT, None, ALU.min)
                ins.then_inc(gu_clamped, 1)
                for n in range(2):
                    ins = dve.tensor_scalar(lin_in[0:TILE, n * 512:(n + 1) * 512], bank[2 + n][0:TILE, :], LIMIT, -LIMIT,
                                            ALU.min, ALU.max)
                ins.then_inc(gu_clamped, 1)

            def gate(j):
                dve.wait_ge(gu_clamped, j * 2 + 2)
                dve.scalar_tensor_tensor(lin_in[0:TILE, :], lin_in[0:TILE, :], 1.0, gate_in[0:TILE, :],
                                         ALU.add, ALU.mult)\
                   .then_inc(lin_gated, 1)
                dve.wait_ge(lin_gated, j + 1)
                dve.wait_ge(sig_ready, j + 1)
                dve.tensor_tensor(lin_in[0:TILE, :], lin_in[0:TILE, :], sig_in[0:TILE, :], ALU.mult).then_inc(act_ready, 1)

            for i in range(SPLIT, GU_CHUNKS):
                split(i, i)
                if i == SPLIT:
                    select(sel_gu, 1, sel_gu_ready, sel_gu_used)

            def job(j, first=False, final=False):
                gu(j, 0)
                if first:
                    dve.wait_ge(xn_stored, 16 * TT)
                    clamp(0, GU_CHUNKS)
                    turned(1, xT_hi, xT_lo, xT_hi_ready, xT_lo_ready)
                gate(j - 1)
                for i in range(1, 4):
                    gu(j, i)
                select(sel_dn, j - 1, sel_dn_ready, sel_dn_used)
                if not final:
                    select(sel_gu, j + 1, sel_gu_ready, sel_gu_used)
                for i in range(4, 7):
                    gu(j, i)
                turned(j - 1, aT_hi, aT_lo, aT_hi_ready, aT_lo_ready)
                gu(j, 7)
                dn(j - 1, 0)
                dn(j - 1, 1)
                clamp(j, gu_chunk(j, GU_CHUNKS - 1) + 1)
                dn(j - 1, 2)
                if final:
                    gate(j)
                else:
                    turned(j + 1, xT_hi, xT_lo, xT_hi_ready, xT_lo_ready)
                dn(j - 1, 3)

            job(1, first=True)
            end = jobs_end(dve)
            with dve.Fori(2, end - 1) as j:
                job(j)
            last = dve.snap(end - 1)
            job(last, final=True)
            turned(last, xT_hi, xT_lo, aT_hi_ready, aT_lo_ready)
            select(sel_dn, last, sel_dn_ready, sel_dn_used)
            for i in range(DN_CHUNKS):
                split(last_dn_chunk(last, i), DN_LAST[i])

            dve.wait_ge(g_fin_loaded, 16)
            for t in range(TT):
                dve.wait_ge(ss_f_ready, t + 1)
                dve.tensor_scalar(std_f[:, t:t + 1], ss_f[:, t:t + 1], 1.0 / D_MODEL, EPS, ALU.mult, ALU.add)\
                   .then_inc(var_f_ready, 1)
                dve.wait_ge(std_f_ready, t + 1)
                dve.reciprocal(rstd_f[:, t:t + 1], std_f[:, t:t + 1]).then_inc(rstd_f_ready, 1)
                dve.wait_ge(rstd_f_ready, t + 1)
                row = raw01[:, t, 0:D_MODEL]
                dve.scalar_tensor_tensor(row, row, rstd_f[:, t:t + 1], g_fin_row[:, :], ALU.mult, ALU.mult)\
                   .then_inc(out_ready, 1)

        @block.tensor
        def _(pe):
            def product(dst, a_hi, a_lo, b_hi, b_lo, start, stop):
                pe.matmul(dst, a_hi, b_hi, start=start, stop=False)
                pe.matmul(dst, a_hi, b_lo, start=False, stop=False)
                return pe.matmul(dst, a_lo, b_hi, start=False, stop=stop)

            for t in range(TT):
                pe.wait_ge(x_loaded[t], 16)
                pe.wait_ge(diag_ready, t + 1)
                for k in range(KD):
                    ins = pe.matmul(bank[k][:, t * P:(t + 1) * P], x_sb[:, t, k * P:(k + 1) * P], diag[:, t, :],
                                    start=t == 0, stop=t == TT - 1)
                    if t == TT - 1:
                        ins.then_inc(xT_turned, 1)

            def project(s, n, first=0, last=KD):
                i = first_tile[s] + n
                if n == 0:
                    pe.wait_ge(front_lo, s + 1)
                if i >= 2:
                    pe.wait_ge(proj_taken, i - 1)
                hi = hi01[:, s % 2, :].rearrange("p (k n) -> p k n", k=KD)
                lo = lo01[:, s % 2, :].rearrange("p (k n) -> p k n", k=KD)
                for k in range(first, last):
                    if i == 0:
                        pe.wait_ge(xnT_lo_ready, k + 1)
                    if chunks[s][0] == "v":
                        cols = slice(n * P, (n + 1) * P)
                        ins = product(bank[i % 2][:, 0:2 * P], xnT_hi[:, k, cols], xnT_lo[:, k, cols],
                                      hi[:, k, :], lo[:, k, :], k == 0, k == KD - 1)
                    else:
                        cols = slice(n * P, (n + 1) * P)
                        ins = product(bank[i % 2][:, :], hi[:, k, cols], lo[:, k, cols],
                                      xnT_hi[:, k, :], xnT_lo[:, k, :], k == 0, k == KD - 1)
                if last == KD:
                    ins.then_inc(proj_ready, 1)

            for s in range(3):
                for n in range(tiles_of[s]):
                    project(s, n)

            def attend(h):
                pair = slice(h // 2 * P, h // 2 * P + P)
                if h:
                    pe.wait_ge(heads_taken, h)
                for c in range(TT):
                    pe.wait_ge(pT_lo_ready, h * TT + c + 1)
                    ins = product(bank[6][:, :], v_hi[:, c, pair], v_lo[:, c, pair], pT_hi[:, c, :], pT_lo[:, c, :],
                                  c == 0, c == TT - 1)
                ins.then_inc(heads_ready, 1)

            def sum_squares(k, ready, number, summed):
                pe.wait_ge(ready, number)
                for t in range(TT):
                    ins = pe.matmul(bank[7][:, t * KD + k:t * KD + k + 1],
                                    sq_sb[:, 0 if k < NA else 1, t * P:(t + 1) * P], ones[:, 0:1], start=True, stop=True)
                ins.then_inc(summed, 1)

            pe.wait_ge(consts_made, 3)
            for h in range(HEADS):
                s = 3 + h
                rows, pair = slice(HEAD_DIM * (h % 2), HEAD_DIM * (h % 2) + HEAD_DIM), h // 2 % 2
                pe.wait_ge(proj_taken, first_tile[[0, 3, 5, 7][h // 2]] + 2)
                for t in range(TT):
                    n = h * TT + t
                    if n >= 2:
                        pe.wait_ge(scores_taken, n - 1)
                    q = slice(t * P, (t + 1) * P)
                    product(bank[2 + t % 2][:, :], qk_hi[rows, pair, 0, q], qk_lo[rows, pair, 0, q],
                            qk_hi[rows, pair, 1, :], qk_lo[rows, pair, 1, :], True, True).then_inc(scores_ready, 1)
                project(s, 0)
                if h:
                    attend(h - 1)
                pe.wait_ge(probs_ready, (h + 1) * TT)
                for c in range(TT):
                    if c == 2:
                        project(s, 1, 0, KD // 2)
                    if h * TT + c >= 2:
                        pe.wait_ge(pT_lo_ready, h * TT + c - 1)
                    for t in range(TT):
                        ins = pe.transpose(bank[4 + c % 2][:, t * P:(t + 1) * P], probs[:, t, c * P:(c + 1) * P],
                                           ident[:, :])
                    ins.then_inc(probs_turned, 1)
                project(s, 1, KD // 2, KD)
                if h in (3, 5, 7):
                    pair_no = (h - 3) // 2
                    sum_squares(pair_no, sq_attn_ready, pair_no + 1, sq_attn_summed)
                if h == 7:
                    sum_squares(NA, sq_conv_ready, 1, sq_conv_summed)
            project(N_IN - 1, 0)
            attend(HEADS - 1)
            project(N_IN - 1, 1)
            sum_squares(NA + 1, sq_conv_ready, 2, sq_conv_summed)
            sum_squares(NA - 1, sq_attn_ready, NA, sq_attn_summed)

            def turn_x1(t):
                pe.wait_ge(mix_taken, 2 * TT + 2 * t + 2)
                for g in range(2):
                    for k in range(TT):
                        ins = pe.transpose(bank[2 * t + g][:, k * P:(k + 1) * P],
                                           x1[:, t, (g * TT + k) * P:(g * TT + k + 1) * P], ident[:, :])
                    ins.then_inc(x1_turned, 1)

            def route(t):
                pe.wait_ge(x1T_act_ready, t + 1)
                pe.wait_ge(x1T_dve_ready, t + 1)
                for k in range(KD):
                    ins = pe.matmul(bank[2 * t][:, 0:E], x1T[:, k, t * P:(t + 1) * P], w_r[:, k, :],
                                    start=k == 0, stop=k == KD - 1)
                ins.then_inc(router_ready, 1)

            for half in range(2):
                if half == 0:
                    pe.wait_ge(proj_taken, first_tile[N_IN])
                    pe.wait_ge(heads_taken, HEADS)
                for c in range(2):
                    s = N_IN + 2 * half + c
                    if s == N_IN:
                        sum_squares(NA + 2, sq_conv_ready, 3, sq_conv_summed)
                    pe.wait_ge(front_lo, s + 1)
                    pe.wait_ge(mT_lo_ready, 4 * half + 2 * c + 2)
                    for t in range(TT):
                        for n in range(2):
                            b = 2 * t + n
                            if s == N_IN and b == 6:
                                sum_squares(NA + 3, sq_conv_ready, NC_, sq_conv_summed)
                            if s == N_IN and b == 7:
                                pe.wait_ge(sums_taken, 1)
                            if half == 1 and c == 0:
                                pe.wait_ge(mix_taken, b + 1)
                            if half == 1 and c == 1 and n == 0 and t >= 2:
                                turn_x1(t - 2)
                            for i in range(2):
                                k, q, cols = 4 * half + 2 * c + i, slice(t * P, (t + 1) * P), \
                                    slice(i * D_MODEL + n * 512, i * D_MODEL + (n + 1) * 512)
                                ins = product(bank[b][:, :], mT_hi[:, k, q], mT_lo[:, k, q], hi01[:, s % 2, cols],
                                              lo01[:, s % 2, cols], c == 0 and i == 0, c == 1 and i == 1)
                            if c == 1:
                                ins.then_inc(mix_ready, 1)
                    if c == 0:
                        ins.then_inc(mix_half_used, 1)

            pe.wait_ge(w_r_ready, 1)
            route(0)
            turn_x1(2)
            route(1)
            turn_x1(3)
            route(2)
            route(3)
            pe.wait_ge(consts_made, 8)
            for t in range(TT):
                pe.wait_ge(mask_ready, t + 1)
                ins = pe.matmul(bank[1][:, t * E:(t + 1) * E], before[:, :], mask[:, t, :], start=t == 0, stop=t == TT - 1)
                if t < TT - 1:
                    pe.matmul(bank[1][:, (t + 1) * E:TT * E], ones[:, :],
                              mask[:, t, :].unsqueeze(1).to_broadcast([P, TT - 1 - t, E]), start=False, stop=False)
                else:
                    ins.then_inc(rank_ready, 1)
            for t in range(TT):
                ins = pe.matmul(bank[5][:, 0:E], ones[:, :], mask[:, t, :], start=t == 0, stop=t == TT - 1)
            ins.then_inc(counts_ready, 1)
            pe.wait_ge(router_ready, TT)
            for t in range(TT):
                pe.wait_ge(pick_ready, t + 1)
                if t < 2:
                    pe.wait_ge(xn_dve_ready, t + 1)
                else:
                    pe.wait_ge(xn_pool_ready, t - 1)
                for k in range(KD):
                    ins = pe.matmul(bank[6 + k // TT][:, (k % TT) * TILE:(k % TT + 1) * TILE], xn[:, t, k * P:(k + 1) * P],
                                    pick[:, t, :], start=t == 0 and k % TT == 0,
                                    stop=t == TT - 1 and k % TT == TT - 1)
                    if t == TT - 1 and k % TT == TT - 1:
                        ins.then_inc(got_turned, 1)
                if t == 1:
                    pe.wait_ge(pick_1_ready, 1 + TT)
                    for u in range(TT):
                        ins = pe.matmul(bank[4][0:TILE, 0:1], pick_1[:, u, :], token_1[:, u:u + 1], start=u == 0,
                                        stop=u == TT - 1)
                    ins.then_inc(places_1_ready, 1)

            def transpose_got(j):
                pe.wait_ge(x_gathered, j * 16)
                turn(x_got, got_turned)

            def turn(src, done):
                for g in range(2):
                    for k in range(TT):
                        ins = pe.transpose(bank[6 + g][:, k * TILE:(k + 1) * TILE],
                                           src[0:TILE, (g * TT + k) * P:(g * TT + k + 1) * P],
                                           ident[0:TILE, 0:TILE])
                    ins.then_inc(done, 1)

            def turn_act(j):
                pe.wait_ge(act_ready, j + 1)
                turn(lin_in, act_turned)

            def bias_gu(j):
                pe.wait_ge(sel_gu_ready, j + 1)
                for n in range(4):
                    ins = pe.matmul(bank[n][0:TILE, :], sel_gu[:, :], b_hl[:, n * 512:(n + 1) * 512], start=True, stop=False)
                ins.then_inc(sel_gu_used, 1)

            def gate_up(m, slot_no, i):
                pe.wait_ge(w_lo_ready, m + 1)
                hi, lo = hi_slot(slot_no % SPLIT), lo_slot(slot_no % SPLIT)
                last = i == GU_CHUNKS - 1
                for a, w, end_ in ((xT_hi, hi, False), (xT_hi, lo, False), (xT_lo, hi, last)):
                    for n in range(4):
                        ins = pe.matmul(bank[n][0:TILE, :], a[:, i, :], w[:, n * 512:(n + 1) * 512], start=False, stop=end_)
                ins.then_inc(w_used, 1)

            def bias_dn(j):
                pe.wait_ge(y_ready, j)
                pe.wait_ge(sel_dn_ready, j + 1)
                for n in range(2):
                    ins = pe.matmul(bank[4 + n][0:TILE, :], sel_dn[:, :], b_hl[:, (4 + n) * 512:(5 + n) * 512],
                                    start=True, stop=False)
                ins.then_inc(sel_dn_used, 1)

            def down(m, slot_no, i, hi_T, lo_T):
                pe.wait_ge(w_lo_ready, m + 1)
                hi, lo = hi_slot(slot_no % SPLIT), lo_slot(slot_no % SPLIT)
                for r in range(2):
                    last = i == DN_CHUNKS - 1 and r == 1
                    for a, w, end_ in ((hi_T, hi, False), (hi_T, lo, False), (lo_T, hi, last)):
                        for n in range(2):
                            ins = pe.matmul(bank[4 + n][0:TILE, :], a[:, 2 * i + r, :],
                                            w[:, r * D_MODEL + n * 512:r * D_MODEL + (n + 1) * 512],
                                            start=False, stop=end_)
                ins.then_inc(w_used, 1)

            pe.wait_ge(b_ready, 1)
            bias_gu(0)
            pe.wait_ge(xT_lo_ready, 2)
            for i in range(GU_CHUNKS):
                gate_up(i, GU0[i], i)
            transpose_got(1)

            def job(j, final=False):
                pe.wait_ge(gu_clamped, j * 2)
                bias_gu(j)
                pe.wait_ge(xT_lo_ready, j * 2 + 2)
                for i in range(GU_CHUNKS):
                    gate_up(gu_chunk(j, i), GU[i], i)
                    if i == 3:
                        turn_act(j - 1)
                pe.wait_ge(aT_lo_ready, j * 2)
                if not final:
                    transpose_got(j + 1)
                bias_dn(j - 1)
                for i in range(DN_CHUNKS):
                    if final and i == DN_CHUNKS - 1:
                        turn_act(j)
                    down(dn_chunk(j - 1, i), DN[i], i, aT_hi, aT_lo)

            job(1)
            end = jobs_end(pe)
            with pe.Fori(2, end - 1) as j:
                job(j)
            last = pe.snap(end - 1)
            job(last, final=True)
            bias_dn(last)
            pe.wait_ge(aT_lo_ready, end * 2)
            for i in range(DN_CHUNKS):
                down(last_dn_chunk(last, i), DN_LAST[i], i, xT_hi, xT_lo)


_INS = ['x', 'mix_norm_g', 'w_in', 'conv_w', 'attn_out_norm_g', 'conv_out_norm_g', 'w_out', 'ffn_norm_g',
        'w_router', 'b_router', 'w_gate_up', 'b_gate_up', 'w_down', 'b_down', 'final_norm_g']
_OUTS = [((1, SEQ, D_MODEL), 'float32')]


def kernel(**inputs):
    import numpy as _np
    import concourse.bacc as _bacc
    from concourse import mybir as _mybir
    from concourse.bass_utils import run_bass_kernel_spmd as _run

    nc = _bacc.Bacc("TRN2", target_bir_lowering=False, num_devices=1)
    arrays, args = {}, []
    for name in _INS:
        a = _np.ascontiguousarray(inputs[name])
        arrays[f"in_{name}_dram"] = a
        args.append(nc.dram_tensor(f"in_{name}_dram", a.shape, _mybir.dt.from_np(a.dtype), kind="ExternalInput").ap())
    for i, (shape, dtype) in enumerate(_OUTS):
        dt = _mybir.dt.from_np(_np.dtype(dtype))
        args.append(nc.dram_tensor(f"out_{i}_dram", shape, dt, kind="ExternalOutput").ap())
    build(nc, *args)
    r = _run(nc, [arrays], core_ids=[0])
    return r.results[0]["out_0_dram"]
```
